# Optimizing a Trainium2 kernel written in Bass

```python
import jax, jax.numpy as jnp
from jax import lax
import numpy as np

D_MODEL = 1024
BATCH = 1
SEQ = 256
DEPTH = 2

CHUNK = 64
LEFT_CHUNKS = 8
BAND = (LEFT_CHUNKS + 1) * CHUNK
HEAD_DIM = 64
N_HEADS_A = 8
N_HEADS_C = 8
WIDTH_A = N_HEADS_A * HEAD_DIM
WIDTH_C = N_HEADS_C * HEAD_DIM
POOL_WINDOWS = (2, 4, 8, 16)
N_POOL_GROUPS = 4
POOL_GROUP_DIM = 128
WIDTH_B = N_POOL_GROUPS * POOL_GROUP_DIM
REL_CLIP = 128
N_REL = 2 * REL_CLIP + 1
N_BRANCHES = 3
D_FF = 2816
Q_BLOCK = 128
N_MOD = 9
EPS = 1e-6
NEG_INF = -1e30

SPLIT_SIZES = (WIDTH_A, WIDTH_A, WIDTH_A, WIDTH_B, WIDTH_C, WIDTH_C, WIDTH_C, N_HEADS_C, N_BRANCHES * D_MODEL)
D_IN = sum(SPLIT_SIZES)
SPLIT_POINTS = tuple(int(p) for p in np.cumsum(SPLIT_SIZES)[:-1])


def rms_norm(x, gain):
    xf = x.astype(jnp.float32)
    y = xf * lax.rsqrt(jnp.mean(xf * xf, axis=-1, keepdims=True) + EPS)
    return (y * gain.astype(jnp.float32)).astype(x.dtype)

def modulate(h, shift, scale):
    return h * (1 + scale[:, None, :]) + shift[:, None, :]

def swiglu(h, w_gate, w_up, w_down):
    return (jax.nn.silu(h @ w_gate) * (h @ w_up)) @ w_down

def chunked_relpos_attention(q, k, v, gq, gk, rel_bias):
    B, S, H, dh = q.shape
    nc = S // CHUNK
    qf = rms_norm(q, gq).astype(jnp.float32) * (dh ** -0.5)
    kf = rms_norm(k, gk).astype(jnp.float32)
    qc = qf.reshape(B, nc, CHUNK, H, dh)
    pad = ((0, 0), (LEFT_CHUNKS * CHUNK, 0), (0, 0), (0, 0))
    kp = jnp.pad(kf, pad).reshape(B, nc + LEFT_CHUNKS, CHUNK, H, dh)
    vp = jnp.pad(v, pad).reshape(B, nc + LEFT_CHUNKS, CHUNK, H, dh)
    band_idx = np.arange(nc)[:, None] + np.arange(LEFT_CHUNKS + 1)[None, :]
    kb = kp[:, band_idx].reshape(B, nc, BAND, H, dh)
    vb = vp[:, band_idx].reshape(B, nc, BAND, H, dh)
    logits = jnp.einsum('bnqhd,bnkhd->bhnqk', qc, kb)
    rel = np.arange(CHUNK)[:, None] + LEFT_CHUNKS * CHUNK - np.arange(BAND)[None, :]
    rel_idx = np.clip(rel, -REL_CLIP, REL_CLIP) + REL_CLIP
    bias = rel_bias[:, rel_idx].astype(jnp.float32)
    valid = np.repeat(band_idx >= LEFT_CHUNKS, CHUNK, axis=1)
    logits = jnp.where(valid[None, None, :, None, :], logits + bias[None, :, None], NEG_INF)
    p = jax.nn.softmax(logits, axis=-1).astype(v.dtype)
    out = jnp.einsum('bhnqk,bnkhd->bnqhd', p, vb)
    return out.reshape(B, S, H * dh)

def multiscale_pool(u, w_pool, pool_scale):
    B, S, _ = u.shape
    uf = u.astype(jnp.float32)
    cs = jnp.concatenate([jnp.zeros((B, 1, WIDTH_B), jnp.float32), jnp.cumsum(uf, axis=1)], axis=1)
    t = jnp.arange(S, dtype=jnp.float32)
    diffs = []
    for g, w in enumerate(POOL_WINDOWS):
        sl = slice(g * POOL_GROUP_DIM, (g + 1) * POOL_GROUP_DIM)
        csg = cs[:, :, sl]
        upper = csg[:, 1:]
        lower = jnp.pad(csg[:, :S + 1 - w], ((0, 0), (w - 1, 0), (0, 0)))
        count = jnp.minimum(t + 1, float(w))[None, :, None]
        diffs.append((upper - lower) / count - uf[:, :, sl])
    d = jnp.stack(diffs, axis=2).astype(u.dtype)
    y = jnp.einsum('bsgc,gce->bsge', d, w_pool).reshape(B, S, WIDTH_B)
    return y * pool_scale

def forgetting_attention(q, k, v, gq, gk, f_logit):
    B, S, H, dh = q.shape
    qf = rms_norm(q, gq).astype(jnp.float32) * (dh ** -0.5)
    kf = rms_norm(k, gk).astype(jnp.float32)
    cum_logf = jnp.cumsum(jax.nn.log_sigmoid(f_logit.astype(jnp.float32)), axis=1)
    cum_k = cum_logf.transpose(0, 2, 1)
    kpos = jnp.arange(S)

    def block(i):
        start = i * Q_BLOCK
        qb = lax.dynamic_slice_in_dim(qf, start, Q_BLOCK, axis=1)
        cq = lax.dynamic_slice_in_dim(cum_k, start, Q_BLOCK, axis=2)
        logits = jnp.einsum('bqhd,bkhd->bhqk', qb, kf) + (cq[..., None] - cum_k[:, :, None, :])
        qpos = start + jnp.arange(Q_BLOCK)
        mask = kpos[None, :] <= qpos[:, None]
        logits = jnp.where(mask[None, None], logits, NEG_INF)
        p = jax.nn.softmax(logits, axis=-1).astype(v.dtype)
        return jnp.einsum('bhqk,bkhd->bqhd', p, v)

    out = lax.map(block, jnp.arange(S // Q_BLOCK))
    return out.transpose(1, 0, 2, 3, 4).reshape(B, S, H * dh)

def hybrid_mixer(h, w_in, qk_gain, rel_bias, forget_bias, w_pool, pool_scale, w_branch, w_out):
    B, S, _ = h.shape
    proj = h @ w_in
    qa, ka, va, ub, qc, kc, vc, f_lin, g_lin = jnp.split(proj, SPLIT_POINTS, axis=-1)
    ha = lambda t: t.reshape(B, S, N_HEADS_A, HEAD_DIM)
    hc = lambda t: t.reshape(B, S, N_HEADS_C, HEAD_DIM)
    ya = chunked_relpos_attention(ha(qa), ha(ka), ha(va), qk_gain[0], qk_gain[1], rel_bias)
    yb = multiscale_pool(ub, w_pool, pool_scale)
    yc = forgetting_attention(hc(qc), hc(kc), hc(vc), qk_gain[2], qk_gain[3], f_lin + forget_bias)
    ys = jnp.stack([ya, yb, yc], axis=2)
    branch = jnp.einsum('bsnw,nwd->bsnd', ys, w_branch)
    gates = jax.nn.sigmoid(g_lin.reshape(B, S, N_BRANCHES, D_MODEL))
    merged = jnp.sum(gates * branch, axis=2)
    return merged @ w_out

def first_inputs(seed: int = 0) -> dict:
    key = jax.random.key(seed)
    ks = jax.random.split(key, 18)
    nrm = lambda k, shape, s: jax.random.normal(k, shape, jnp.float32) * s
    return {
        "x": nrm(ks[0], (BATCH, SEQ, D_MODEL), 1.0),
        "c": nrm(ks[1], (BATCH, D_MODEL), 1.0),
        "w_ada": nrm(ks[2], (DEPTH, D_MODEL, N_MOD * D_MODEL), 0.5 * D_MODEL ** -0.5),
        "b_ada": nrm(ks[3], (DEPTH, N_MOD * D_MODEL), 0.02),
        "norm_gain": 1.0 + nrm(ks[4], (DEPTH, 3, D_MODEL), 0.05),
        "ffn_w_gate": nrm(ks[5], (DEPTH, 2, D_MODEL, D_FF), D_MODEL ** -0.5),
        "ffn_w_up": nrm(ks[6], (DEPTH, 2, D_MODEL, D_FF), D_MODEL ** -0.5),
        "ffn_w_down": nrm(ks[7], (DEPTH, 2, D_FF, D_MODEL), D_FF ** -0.5),
        "w_in": nrm(ks[8], (DEPTH, D_MODEL, D_IN), D_MODEL ** -0.5),
        "qk_gain": 1.0 + nrm(ks[9], (DEPTH, 4, HEAD_DIM), 0.05),
        "rel_bias": nrm(ks[10], (DEPTH, N_HEADS_A, N_REL), 0.5),
        "forget_bias": 1.0 + 3.0 * jax.random.uniform(ks[11], (DEPTH, N_HEADS_C), jnp.float32),
        "w_pool": nrm(ks[12], (DEPTH, N_POOL_GROUPS, POOL_GROUP_DIM, POOL_GROUP_DIM), POOL_GROUP_DIM ** -0.5),
        "pool_scale": 1.0 + nrm(ks[13], (DEPTH, WIDTH_B), 0.05),
        "w_branch": nrm(ks[14], (DEPTH, N_BRANCHES, WIDTH_A, D_MODEL), WIDTH_A ** -0.5),
        "w_out": nrm(ks[15], (DEPTH, D_MODEL, D_MODEL), D_MODEL ** -0.5),
    }

def first_block(x, c, w_ada, b_ada, norm_gain, ffn_w_gate, ffn_w_up, ffn_w_down, w_in, qk_gain,
              rel_bias, forget_bias, w_pool, pool_scale, w_branch, w_out):
    B = x.shape[0]
    c_act = jax.nn.silu(c)
    for l in range(DEPTH):
        mod = (c_act @ w_ada[l] + b_ada[l]).reshape(B, N_MOD, D_MODEL)
        h = modulate(rms_norm(x, norm_gain[l, 0]), mod[:, 0], mod[:, 1])
        x = x + 0.5 * mod[:, 2][:, None, :] * swiglu(h, ffn_w_gate[l, 0], ffn_w_up[l, 0], ffn_w_down[l, 0])
        h = modulate(rms_norm(x, norm_gain[l, 1]), mod[:, 3], mod[:, 4])
        x = x + mod[:, 5][:, None, :] * hybrid_mixer(h, w_in[l], qk_gain[l], rel_bias[l], forget_bias[l],
                                                      w_pool[l], pool_scale[l], w_branch[l], w_out[l])
        h = modulate(rms_norm(x, norm_gain[l, 2]), mod[:, 6], mod[:, 7])
        x = x + 0.5 * mod[:, 8][:, None, :] * swiglu(h, ffn_w_gate[l, 1], ffn_w_up[l, 1], ffn_w_down[l, 1])
    return x


HEADS_PER_GROUP = 8
DILATION_GROUPS = ((128, 1), (512, 4), (2048, 16))
N_GROUPS = len(DILATION_GROUPS)
N_ATTN_HEADS = N_GROUPS * HEADS_PER_GROUP
QKV_WIDTH = N_ATTN_HEADS * HEAD_DIM
ATTN_OUT = HEADS_PER_GROUP * HEAD_DIM
CONV_WIDTH = D_MODEL
CONV_K = 3
D_FF_2 = ((8 * D_MODEL // 3) + 127) // 128 * 128
IN_WIDTH = 3 * QKV_WIDTH + 3 * CONV_WIDTH + 2 * D_MODEL
NUM_BUCKETS = 32
MAX_DISTANCE = 2048
BLOCK = 128
N_SUB = 3
NEG_INF_2 = -1e30


def _t5_bucket(dist):
    exact = NUM_BUCKETS // 2
    d = np.maximum(dist, 1).astype(np.float32)
    large = exact + (np.log(d / exact) / np.log(MAX_DISTANCE / exact) * (NUM_BUCKETS - exact)).astype(np.int32)
    large = np.minimum(large, NUM_BUCKETS - 1)
    return np.where(dist < exact, dist, large).astype(np.int32)

def _rmsnorm(x, g):
    xf = x.astype(jnp.float32)
    y = xf * lax.rsqrt(jnp.mean(xf * xf, axis=-1, keepdims=True) + EPS) * g.astype(jnp.float32)
    return y.astype(x.dtype)

def _swiglu(h, w_gate, w_up, w_down):
    return (jax.nn.silu(h @ w_gate) * (h @ w_up)) @ w_down

def _causal_dwconv(u, w):
    rhs = w.astype(u.dtype).reshape(CONV_K, 1, u.shape[-1])
    return lax.conv_general_dilated(u, rhs, window_strides=(1,), padding=[(CONV_K - 1, 0)],
                                    dimension_numbers=("NWC", "WIO", "NWC"),
                                    feature_group_count=u.shape[-1])

def _dilated_window_attention(q, k, v, bias_tab, window, dilation):
    B, S, H, E = q.shape
    span = window // dilation
    L = S // dilation
    nb = -(-L // BLOCK)
    Lp = nb * BLOCK

    def to_sub(t):
        t = t.reshape(B, L, dilation, H, E)
        return jnp.pad(t, ((0, 0), (0, Lp - L), (0, 0), (0, 0), (0, 0)))

    qs, ks, vs = to_sub(q), to_sub(k), to_sub(v)
    qb = qs.reshape(B, nb, BLOCK, dilation, H, E)

    def key_blocks(t):
        tp = jnp.pad(t, ((0, 0), (BLOCK, 0), (0, 0), (0, 0), (0, 0)))
        prev = tp[:, :Lp].reshape(B, nb, BLOCK, dilation, H, E)
        cur = t.reshape(B, nb, BLOCK, dilation, H, E)
        return jnp.concatenate([prev, cur], axis=2)

    kb, vb = key_blocks(ks), key_blocks(vs)

    i = np.arange(BLOCK)[:, None]
    j = np.arange(2 * BLOCK)[None, :]
    rel = i - j + BLOCK
    band = (rel >= 0) & (rel <= span)
    first_ok = (np.arange(nb)[:, None, None] > 0) | (j[None] >= BLOCK)
    mask = jnp.asarray(band[None] & first_ok)[None, :, None, None]
    bucket = jnp.asarray(_t5_bucket(np.maximum(rel, 0) * dilation))
    bias = jnp.transpose(bias_tab[bucket].astype(jnp.float32), (2, 0, 1))

    logits = jnp.einsum("bnqrhe,bnkrhe->bnrhqk", qb, kb).astype(jnp.float32) * (HEAD_DIM ** -0.5)
    logits = jnp.where(mask, logits + bias, NEG_INF_2)
    m = jnp.max(logits, axis=-1, keepdims=True)
    p = jnp.exp(logits - m)
    s = jnp.sum(p, axis=-1)
    o = jnp.einsum("bnrhqk,bnkrhe->bnqrhe", p, vb.astype(jnp.float32))
    s_q = jnp.transpose(s, (0, 1, 4, 2, 3))
    o = o / s_q[..., None]
    lse = jnp.transpose(m[..., 0] + jnp.log(s), (0, 1, 4, 2, 3))
    o = o.reshape(B, Lp, dilation, H, E)[:, :L].reshape(B, S, H, E)
    lse = lse.reshape(B, Lp, dilation, H)[:, :L].reshape(B, S, H)
    return o, lse

def _mixer(h, w_in, conv_w, w_conv_out, w_attn_out, w_o, rel_bias):
    B, S, _ = h.shape
    u = h @ w_in
    splits = np.cumsum([QKV_WIDTH, QKV_WIDTH, QKV_WIDTH, CONV_WIDTH, CONV_WIDTH, CONV_WIDTH, D_MODEL])
    q, k, v, cb, cc, ch, g_conv, g_attn = jnp.split(u, splits, axis=-1)

    y_conv = (cb * _causal_dwconv(cc * ch, conv_w)) @ w_conv_out

    q = q.reshape(B, S, N_GROUPS, HEADS_PER_GROUP, HEAD_DIM)
    k = k.reshape(B, S, N_GROUPS, HEADS_PER_GROUP, HEAD_DIM)
    v = v.reshape(B, S, N_GROUPS, HEADS_PER_GROUP, HEAD_DIM)
    outs, lses = [], []
    for g, (window, dilation) in enumerate(DILATION_GROUPS):
        tab = rel_bias[:, g * HEADS_PER_GROUP:(g + 1) * HEADS_PER_GROUP]
        o_g, lse_g = _dilated_window_attention(q[:, :, g], k[:, :, g], v[:, :, g], tab, window, dilation)
        outs.append(o_g)
        lses.append(lse_g)
    alpha = jax.nn.softmax(jnp.stack(lses, axis=0), axis=0)
    o = jnp.sum(alpha[..., None] * jnp.stack(outs, axis=0), axis=0)
    y_attn = o.reshape(B, S, ATTN_OUT).astype(h.dtype) @ w_attn_out

    merged = jax.nn.sigmoid(g_conv) * y_conv + jax.nn.sigmoid(g_attn) * y_attn
    return merged @ w_o

def second_inputs(seed: int = 0) -> dict:
    key = jax.random.key(seed)
    ks = jax.random.split(key, 16)
    f32 = jnp.float32

    def nrm(k, shape, fan_in):
        return jax.random.normal(k, shape, f32) * (fan_in ** -0.5)

    return {
        "x": jax.random.normal(ks[0], (BATCH, SEQ, D_MODEL), f32),
        "c": jax.random.normal(ks[1], (BATCH, D_MODEL), f32),
        "ada_w": nrm(ks[2], (DEPTH, D_MODEL, N_SUB * 3 * D_MODEL), D_MODEL),
        "ada_b": 0.02 * jax.random.normal(ks[3], (DEPTH, N_SUB * 3 * D_MODEL), f32),
        "norm_g": 1.0 + 0.05 * jax.random.normal(ks[4], (DEPTH, N_SUB, D_MODEL), f32),
        "ffn_w_gate": nrm(ks[5], (DEPTH, 2, D_MODEL, D_FF_2), D_MODEL),
        "ffn_w_up": nrm(ks[6], (DEPTH, 2, D_MODEL, D_FF_2), D_MODEL),
        "ffn_w_down": nrm(ks[7], (DEPTH, 2, D_FF_2, D_MODEL), D_FF_2),
        "w_in": nrm(ks[8], (DEPTH, D_MODEL, IN_WIDTH), D_MODEL),
        "conv_w": nrm(ks[9], (DEPTH, CONV_K, CONV_WIDTH), CONV_K),
        "w_conv_out": nrm(ks[10], (DEPTH, CONV_WIDTH, D_MODEL), CONV_WIDTH),
        "w_attn_out": nrm(ks[11], (DEPTH, ATTN_OUT, D_MODEL), ATTN_OUT),
        "w_o": nrm(ks[12], (DEPTH, D_MODEL, D_MODEL), D_MODEL),
        "rel_bias": 0.5 * jax.random.normal(ks[13], (NUM_BUCKETS, N_ATTN_HEADS), f32),
        "final_g": 1.0 + 0.05 * jax.random.normal(ks[14], (D_MODEL,), f32),
    }

def second_block(x, c, ada_w, ada_b, norm_g, ffn_w_gate, ffn_w_up, ffn_w_down, w_in, conv_w,
              w_conv_out, w_attn_out, w_o, rel_bias, final_g):
    cs = jax.nn.silu(c)
    B = c.shape[0]
    for l in range(DEPTH):
        mod = (cs @ ada_w[l] + ada_b[l]).reshape(B, N_SUB, 3, D_MODEL)[:, :, :, None, :]
        h = _rmsnorm(x, norm_g[l, 0]) * (1.0 + mod[:, 0, 1]) + mod[:, 0, 0]
        x = x + 0.5 * mod[:, 0, 2] * _swiglu(h, ffn_w_gate[l, 0], ffn_w_up[l, 0], ffn_w_down[l, 0])
        h = _rmsnorm(x, norm_g[l, 1]) * (1.0 + mod[:, 1, 1]) + mod[:, 1, 0]
        x = x + mod[:, 1, 2] * _mixer(h, w_in[l], conv_w[l], w_conv_out[l], w_attn_out[l], w_o[l], rel_bias)
        h = _rmsnorm(x, norm_g[l, 2]) * (1.0 + mod[:, 2, 1]) + mod[:, 2, 0]
        x = x + 0.5 * mod[:, 2, 2] * _swiglu(h, ffn_w_gate[l, 1], ffn_w_up[l, 1], ffn_w_down[l, 1])
    return _rmsnorm(x, final_g)


def setup_inputs(seed=0):
    out = dict(first_inputs(seed))
    for name, value in second_inputs(seed + 1).items():
        if name != "x":
            out[name + "_2"] = value
    return out


def reference(
    x, c, w_ada, b_ada, norm_gain, ffn_w_gate, ffn_w_up, ffn_w_down, w_in, qk_gain, rel_bias,
    forget_bias, w_pool, pool_scale, w_branch, w_out, c_2, ada_w_2, ada_b_2, norm_g_2,
    ffn_w_gate_2, ffn_w_up_2, ffn_w_down_2, w_in_2, conv_w_2, w_conv_out_2, w_attn_out_2, w_o_2,
    rel_bias_2, final_g_2,
):
    x = first_block(
        x, c, w_ada, b_ada, norm_gain, ffn_w_gate, ffn_w_up, ffn_w_down, w_in, qk_gain,
        rel_bias, forget_bias, w_pool, pool_scale, w_branch, w_out,
    )
    return second_block(
        x, c_2, ada_w_2, ada_b_2, norm_g_2, ffn_w_gate_2, ffn_w_up_2, ffn_w_down_2, w_in_2,
        conv_w_2, w_conv_out_2, w_attn_out_2, w_o_2, rel_bias_2, final_g_2,
    )


_drawn_inputs = setup_inputs


def setup_inputs(seed=0):
    import zlib

    import numpy as np

    out = dict(_drawn_inputs(seed))
    spreads = {}
    factors = {'qk_gain': 7.405, 'pool_scale': 3.37}
    for name, (base, spread) in spreads.items():
        noise = np.random.default_rng([zlib.crc32(name.encode()), seed]).standard_normal(out[name].shape)
        drawn = base * np.exp(spread * noise) if base else spread * noise
        out[name] = __import__('jax').numpy.asarray(drawn.astype(out[name].dtype))
    for name, factor in factors.items():
        out[name] = (out[name] * factor).astype(out[name].dtype)
    return out
```

```python
from contextlib import ExitStack

import numpy as np

import concourse.bass as bass
from concourse import mybir

F32 = mybir.dt.float32
F32R = mybir.dt.float32r
BF16 = mybir.dt.bfloat16
ALU = mybir.AluOpType
ACT = mybir.ActivationFunctionType
AX_X = mybir.AxisListType.X

P = 128
D = 1024
DT = D // P
S = 256
TT = S // P
DEPTH = 2
D_FF = 2816
TRIPS = D_FF // 256
HEAD = 64
GROUPS2 = 3
REL = 257
TAB = 384
EPS = 1e-6
NEG = -1e30
POOL_W = (2, 4, 8, 16)

FFN_CHUNKS = 3 * TRIPS
MIX = FFN_CHUNKS
MIX_CHUNKS = (36, 48)
LAYER_CHUNKS = tuple(2 * FFN_CHUNKS + m for m in MIX_CHUNKS)
COLS = (2 * 2 * TRIPS + 26, 2 * 2 * TRIPS + 38)
UNITS = 12
FIRST_SUMMED = (0, 1, 3, 4, 6, 7, 9, 10)
FIRST_RING = 5
HEADS = (16, 8)

A_Q, A_K, A_V, B_U, C_Q, C_K, C_V, F_LIN, G_LIN = 0, 512, 1024, 1536, 2048, 2560, 3072, 3584, 3592
MIX1 = ([("u", B_U + 256 * i) for i in range(2)] + [("gb", G_LIN + D + 256 * i) for i in range(4)]
        + [("wb", i) for i in range(2)]
        + [("q", A_Q + 256 * i) for i in range(2)] + [("k", A_K + 256 * i) for i in range(2)]
        + [("v", A_V + 256 * i) for i in range(2)]
        + [("q", C_Q + 256 * i) for i in range(2)] + [("k", C_K + 256 * i) for i in range(2)]
        + [("v", C_V + 256 * i) for i in range(2)]
        + [("g", G_LIN + 256 * i) for i in range(4)] + [("g", G_LIN + 2 * D + 256 * i) for i in range(4)]
        + [("wa", i) for i in range(2)] + [("wc", i) for i in range(2)] + [("wo", i) for i in range(4)])
QKV2 = 1536
CONV2 = 3 * QKV2
MIX2 = ([(n, CONV2 + o + 256 * i) for i in range(4) for n, o in (("cc", D), ("ch", 2 * D))]
        + [("cb", CONV2 + 256 * i) for i in range(4)] + [("gc", CONV2 + 3 * D + 256 * i) for i in range(4)]
        + [("wconv", i) for i in range(4)]
        + [("q", 256 * i) for i in range(6)] + [("k", QKV2 + 256 * i) for i in range(6)]
        + [("v", 2 * QKV2 + 256 * i) for i in range(6)]
        + [("g", CONV2 + 4 * D + 256 * i) for i in range(4)]
        + [("wattn", i) for i in range(2)] + [("wo", i) for i in range(4)])
MIXES = (MIX1, MIX2)
ROW_KINDS = ("wb", "wa", "wc", "wo", "wconv", "wattn")
TOKEN_KINDS = ("u", "v")
assert all(len(m) == c for m, c in zip(MIXES, MIX_CHUNKS))


def column_no(b, k):
    return 2 * TRIPS + sum(kind not in ROW_KINDS for kind, _ in MIXES[b][:k])


def head_no(k):
    return k - 8 if k < 12 else k - 10


UNIT_BEHIND = ((3, 5, 7, 9, 11, 13, 15, 17, 19, 29, 31, 33), (2, 5, 8, 11, 14, 17, 20, 23, 26, 29, 32, 35))


def unit_behind(b, k):
    return UNIT_BEHIND[b].index(k) if k in UNIT_BEHIND[b] else None


GAIN, QKG, POOLS, CONVW, CVEC = 0, 104, 112, 120, 168
PARAMS = 184
NOW_GAIN, NOW_BIAS, NOW_QK, NOW_POOL, NOW_CONV, NOW_C, NOW = 0, 24, 96, 100, 104, 128, 136
ID, ONES, BLOCK, UPTO, CAUSAL, CONSTS = 0, 128, 256, 384, 640, 896


class Signal:

    def __init__(self, sem, per, start=0):
        self.sem, self.start, self.per = sem, start, per

    def at(self, where, k, extra=None):
        if where == "start":
            return k
        if where == "end":
            return self.start + DEPTH * sum(self.per) + k
        b, l = where
        value = l * self.per[b] + (self.start + (DEPTH * self.per[0] if b else 0) + k)
        return value if extra is None else value + extra


def build(nc, t, out):
    ctx = ExitStack()
    with ctx:
        def sb(name, shape, dt=F32):
            return ctx.enter_context(nc.sbuf_tensor(name, shape, dt))

        def ps(name, shape):
            return ctx.enter_context(nc.psum_tensor(name, shape, F32))

        def signal(name, per, start=0):
            return Signal(ctx.enter_context(nc.semaphore(name)), per, start)

        x = sb("x", [P, DT, S])
        h_high = sb("h_high", [P, DT, S], F32R)
        h_low = sb("h_low", [P, DT, S], F32R)
        work = sb("work", [P, DT, S])
        raw = sb("raw", [P, 3, 2048])
        w_high = sb("w_high", [P, 3, 2048], F32R)
        w_low = sb("w_low", [P, 3, 2048], F32R)
        ada_raw = sb("ada_raw", [P, 2, 2048])
        y_high = sb("y_high", [P, 8, S], F32R)
        y_low = sb("y_low", [P, 8, S], F32R)
        proj = sb("proj", [P, 32, S])
        tok = sb("tok", [P, TT, 1536])
        temp = sb("temp", [P, 1152])
        probs_t = sb("probs_t", [P, 1152])
        bias_t = sb("bias_t", [P, 2, 768])
        root = sb("root", [P, 512])
        rstd = sb("rstd", [P, 512])
        const = sb("const", [P, CONSTS])
        params = sb("params", [P, PARAMS])
        ada_bias = sb("ada_bias", [P, 4 * 72])
        now = sb("now", [P, NOW])
        c_act = sb("c_act", [P, 5, DT])
        mod_raw = sb("mod_raw", [P, 24])
        mod = sb("mod", [P, 24])
        mod_a = sb("mod_a", [P, DT])
        mod_g = sb("mod_g", [P, DT])
        eps = sb("eps", [P, 1])
        ones = sb("ones", [P, 1])
        zeros = sb("zeros", [P, 512], BF16)
        f_raw = sb("f_raw", [P, DT, 8])
        f_high = sb("f_high", [P, DT, 8], F32R)
        f_low = sb("f_low", [P, DT, 8], F32R)
        f_bias = sb("f_bias", [P, DEPTH, 8])
        f_val = sb("f_val", [P, TT, 8])
        f_abs = sb("f_abs", [P, TT, 8])
        logf = sb("logf", [P, TT, 8])
        cum_q = sb("cum_q", [P, TT, 8])
        cum_k = root[0:8, S:2 * S]
        neg_top = sb("neg_top", [P, 2])
        total = sb("total", [P, 2])
        share = sb("share", [P, 2])

        ident = const[:, ID:ID + P]
        mean_all = const[:, ONES:ONES + P]
        mean_head = const[:, BLOCK:BLOCK + P]
        upto = const[:, UPTO:UPTO + S]
        causal = const[:, CAUSAL:CAUSAL + S]
        flat = lambda a: a.rearrange("p a b -> p (a b)")
        proj_f, temp_f, work_f = flat(proj[:, :, :]), temp[:, :], flat(work[:, :, :])

        pair = [ps(f"pair{i}", [P, 512]) for i in range(2)]
        small = ps("small", [P, 512])
        stat = ps("stat", [P, 512])
        acc = ps("acc", [P, 2048])
        scores_b, scores_a = acc[:, 0:768], acc[:, 1024:1408]
        turned = [acc[:, 1536:1920], stat[:, 0:384]]

        third = tuple(16 * n // 3 for n in LAYER_CHUNKS)
        raw_landed = [signal(f"raw_landed{i}", third, 32) for i in range(3)]
        w_high_ready = signal("w_high_ready", LAYER_CHUNKS)
        w_low_ready = signal("w_low_ready", LAYER_CHUNKS, 3)
        chunk_used = signal("chunk_used", LAYER_CHUNKS, 3)
        pair_free = [signal(f"pair_free{i}", tuple(c // 2 for c in COLS), 1) for i in range(2)]
        acc_done = signal("acc_done", (3 * 6, 3 * 5))
        acc_taken = signal("acc_taken", (12, 8))
        ada_landed = [signal(f"ada_landed{i}", (16 * 18,) * 2, 16 * 3) for i in range(2)]
        ada_part = signal("ada_part", (8 * 36, 8 * 36), 8 * len(FIRST_SUMMED))
        ada_used = signal("ada_used", (36, 36), 2 + UNITS)
        ada_copied = signal("ada_copied", (36, 36), 2 + UNITS)
        x_ready = signal("x_ready", (24, 24), 8)
        now_ready = signal("now_ready", (2, 2))
        mod_summed = signal("mod_summed", (3, 3))
        mod_ready = signal("mod_ready", (3, 3))
        squares_ready = signal("squares_ready", (24, 24))
        stat_done = signal("stat_done", (3, 3))
        root_ready = signal("root_ready", (3, 3))
        rstd_ready = signal("rstd_ready", (3, 3))
        scaled_ready = signal("scaled_ready", (24, 24))
        h_high_ready = signal("h_high_ready", (24, 24))
        h_ready = signal("h_ready", (24, 24))
        hidden_high = signal("hidden_high", (22, 22))
        hidden_split = signal("hidden_split", (22, 22))
        scores_done = signal("scores_done", tuple(2 * n for n in HEADS))
        logits_ready = signal("logits_ready", tuple(2 * n for n in HEADS))
        exp_ready = signal("exp_ready", tuple(2 * n for n in HEADS))
        probs_ready = signal("probs_ready", tuple(2 * n for n in HEADS))
        turned_done = signal("turned_done", tuple(3 * n for n in HEADS))
        turned_ready = signal("turned_ready", tuple(3 * n for n in HEADS))
        out_done = signal("out_done", HEADS)
        y_high_ready = signal("y_high_ready", HEADS)
        y_ready = signal("y_ready", HEADS)
        bias_landed = [signal(f"bias_landed{i}", (64, 64)) for i in range(2)]
        chain = signal("chain", (2 + 8 * 5 + 8 * 4, 8 * 4 + 4 * 2))
        step_act = signal("step_act", (2, 0))
        side_landed = signal("side_landed", (48, 0))
        pool_d_done = signal("pool_d_done", (1, 0))
        pool_d_ready = signal("pool_d_ready", (4, 0))
        pool_y_done = signal("pool_y_done", (1, 0))
        pool_high = signal("pool_high", (4, 0))
        pool_ready = signal("pool_ready", (4, 0))
        head_sq = signal("head_sq", (8, 0))
        head_stat = signal("head_stat", (8, 0))
        head_root = signal("head_root", (8, 0))
        head_rstd = signal("head_rstd", (8, 0))
        head_normed = signal("head_normed", (8, 0))
        f_split = signal("f_split", (2, 0))
        f_done = signal("f_done", (1, 0))
        f_ready = signal("f_ready", (1, 0))
        cum_done = signal("cum_done", (2, 0))
        cum_ready = signal("cum_ready", (2, 0))
        gates_ready = signal("gates_ready", (2, 1))
        merged_ready = signal("merged_ready", (8, 4))
        out_high_ready = signal("out_high_ready", (4, 4))
        out_split = signal("out_split", (4, 4))
        conv_ready = signal("conv_ready", (0, 4))
        conv_high = signal("conv_high", (0, 4))
        conv_split = signal("conv_split", (0, 4))
        slot_seen = signal("slot_seen", (2, 2))
        const_landed = signal("const_landed", (0, 0))
        rows_landed = signal("rows_landed", (0, 0))
        x_landed = signal("x_landed", (0, 0))
        table_landed = signal("table_landed", (0, 0))
        zeros_ready = signal("zeros_ready", (0, 0))
        params_turned = signal("params_turned", (0, 0))
        params_ready = signal("params_ready", (0, 0))
        table_ready = signal("table_ready", (0, 0))
        table_stored = signal("table_stored", (0, 0))
        x_turned = signal("x_turned", (0, 0))
        c_ready = signal("c_ready", (0, 0))
        result_turned = signal("result_turned", (0, 0))
        result_ready = signal("result_ready", (0, 0))
        result_stored = signal("result_stored", (0, 0))

        ada_cols = t["w_ada_all"].rearrange("l (k p) n -> l p k n", p=P)
        gate_cols = t["ffn_gate_all"].rearrange("l i (k p) n -> l i p k n", p=P)
        up_cols = t["ffn_up_all"].rearrange("l i (k p) n -> l i p k n", p=P)
        down_rows = t["ffn_down_all"].rearrange("l i (c k p) n -> l i c p k n", p=P, k=2)
        in_cols = [t["w_in"].rearrange("l (k p) n -> l p k n", p=P),
                   t["w_in_2"].rearrange("l (k p) n -> l p k n", p=P)]
        rows = lambda a: a.rearrange("l (c k p) n -> l c p k n", p=P, k=2)
        branch_rows = t["w_branch"].rearrange("l b (c k p) n -> l b c p k n", p=P, k=2)
        table_store = nc.dram_tensor("table_store", (40, P, TAB), F32, kind="Internal").ap()
        table_rows = bass.AP(tensor=table_store.tensor, offset=P - 1,
                             ap=[[P * TAB, 40], [TAB - 1, P], [1, S]])
        table_groups = bass.AP(tensor=table_store.tensor, offset=P - 1 + 16 * P * TAB,
                               ap=[[P * TAB, 8], [TAB - 1, P], [8 * P * TAB, 3], [1, S]])

        block = ctx.enter_context(nc.Block())

        def cols3(a):
            return a.rearrange("p (k n) -> p k n", k=8)

        def rows3(a):
            return a.rearrange("p (k n) -> p k n", k=2)

        def conv_u():
            return proj_f[:, 0:DT * (S + 2)].rearrange("p (d n) -> p d n", d=DT)

        def wait_taken(eng, at, b, k):
            q = column_no(b, k)
            eng.wait_ge(pair_free[q % 2].sem, pair_free[q % 2].at(at, q // 2 + 1))

        first_slots = ([(ada_raw[:, i, :], ada_landed[i]) for i in range(2)]
                       + [(raw[:, i, :], raw_landed[i]) for i in range(3)])

        @block.sync
        def _(sp):
            def load(at, n, slot, src, extra=None, split=8, settle=False):
                sp.wait_ge(w_low_ready.sem, w_low_ready.at(at, n - 2, extra))
                if settle:
                    sp.sem_inc(slot_seen.sem, 1)
                dst = raw[:, slot, :]
                sp.dma_start(cols3(dst) if split == 8 else rows3(dst), src).then_inc(raw_landed[slot].sem, 16)

            def load_ada(at, u, slot, src, extra=None):
                sp.wait_ge(ada_used.sem, ada_used.at(at, u - 1, extra))
                sp.dma_start(cols3(ada_raw[:, slot, :]), src).then_inc(ada_landed[slot].sem, 16)

            sp.dma_start(flat(proj[:, 16:24, :])[0:120, 0:P], t["rows_a"]).then_inc(rows_landed.sem, 16)
            sp.dma_start(flat(proj[:, 16:24, :])[0:64, P:2 * P], t["rows_b"]).then_inc(rows_landed.sem, 16)
            sp.dma_start(const[:, :], t["const"]).then_inc(const_landed.sem, 16)
            for u in range(UNITS):
                if u >= FIRST_RING:
                    sp.wait_ge(ada_used.sem, 2 + u - FIRST_RING + 1)
                sp.dma_start(cols3(first_slots[u % FIRST_RING][0]), ada_cols[0, :, :, u * 256:u * 256 + 256]
                             ).then_inc(first_slots[u % FIRST_RING][1].sem, 16)
            sp.wait_ge(ada_used.sem, 2 + 10)
            load((0, 0), 0, 0, gate_cols[0, 0, :, :, 0:256])
            load((0, 0), 1, 1, up_cols[0, 0, :, :, 0:256])
            for b in range(2):
                with sp.Fori(0, DEPTH) as l:
                    at = (b, l)

                    def ada_src(stage, u, extra=None):
                        g = (stage + 1) % 3
                        first = g * 3 * D + u * 256
                        if stage < 2:
                            layer = l + 2 * b
                        else:
                            layer = 3 if b else l + 1
                        start = first if extra is None else extra + first
                        return ada_cols[layer, :, :, bass.ds(start, 256)]

                    def ffn_loads(i):
                        stage, c = 2 * i, i * (MIX + MIX_CHUNKS[b])
                        if i == 1:
                            load(at, c, 0, gate_cols[l + 2 * b, i, :, :, 0:256])
                            load(at, c + 1, 1, up_cols[l + 2 * b, i, :, :, 0:256])
                        load_ada(at, 12 * stage, 0, ada_src(stage, 0))
                        with sp.Fori(0, (TRIPS - 1) // 2) as r:
                            for half in range(2):
                                first = r * 512 + 256 * (1 + half)
                                load(at, c + 2 + 3 * half, 2, gate_cols[l + 2 * b, i, :, :, bass.ds(first, 256)], r * 6)
                                load(at, c + 3 + 3 * half, 0, up_cols[l + 2 * b, i, :, :, bass.ds(first, 256)], r * 6)
                                load(at, c + 4 + 3 * half, 1, down_rows[l + 2 * b, i, r * 2 + half], r * 6, split=2)
                                load_ada(at, 12 * stage + 1 + half, (1 + half) % 2,
                                         ada_src(stage, 1 + half, r * 512), r * 2)
                        load_ada(at, 12 * stage + UNITS - 1, 1, ada_src(stage, UNITS - 1))
                        load(at, c + FFN_CHUNKS - 1, 2, down_rows[l + 2 * b, i, TRIPS - 1], split=2)
                        if i == 1:
                            follow = 3 if b else l + 1
                            load(at, LAYER_CHUNKS[b], 0, gate_cols[follow, 0, :, :, 0:256])
                            load(at, LAYER_CHUNKS[b] + 1, 1, up_cols[follow, 0, :, :, 0:256])

                    ffn_loads(0)
                    for k, (kind, a) in enumerate(MIXES[b]):
                        if kind in ROW_KINDS:
                            src = {"wb": lambda: branch_rows[l, 1, a], "wa": lambda: branch_rows[l, 0, a],
                                   "wc": lambda: branch_rows[l, 2, a],
                                   "wo": lambda: rows(t["w_o_2"] if b else t["w_out"])[l, a],
                                   "wconv": lambda: rows(t["w_conv_out_2"])[l, a],
                                   "wattn": lambda: rows(t["w_attn_out_2"])[l, a]}[kind]()
                            load(at, MIX + k, k % 3, src, split=2, settle=a == 0)
                        else:
                            load(at, MIX + k, k % 3, in_cols[b][l, :, :, a:a + 256], settle=a == 0)
                        u = unit_behind(b, k)
                        if u is not None:
                            load_ada(at, 12 + u, u % 2, ada_src(1, u))
                    ffn_loads(1)
            sp.wait_ge(result_ready.sem, 4)
            sp.dma_start(out.rearrange("b (t p) n -> p (b t) n", p=P),
                         proj_f[:, 0:2 * D].rearrange("p (t n) -> p t n", t=TT)).then_inc(result_stored.sem, 16)
            sp.wait_ge(result_stored.sem, 16)

        @block.scalar
        def _(act):
            def high(at, n, slot, extra=None):
                turn = raw_landed[slot].at(at, 16 * (n // 3 + 1), None if extra is None else extra * 32)
                act.wait_ge(raw_landed[slot].sem, turn)
                act.wait_ge(chunk_used.sem, chunk_used.at(at, n - 2, None if extra is None else extra * 6))
                nc.scalar.activation(w_high[:, slot, :], raw[:, slot, :], ACT.Copy).then_inc(w_high_ready.sem, 1)

            def copy_ada(at, u, parity, dst, extra=None):
                act.wait_ge(ada_used.sem, ada_used.at(at, u + 1, extra) if at != "start" else u + 3)
                nc.scalar.activation(dst, small[:, 2 * parity:2 * parity + 2], ACT.Copy).then_inc(ada_copied.sem, 1)

            def squares(at, s):
                for d in range(DT):
                    act.wait_ge(x_ready.sem, x_ready.at(at, DT * (s - 1) + d + 1))
                    nc.scalar.activation(work[:, d, :], x[:, d, :], ACT.Square).then_inc(squares_ready.sem, 1)

            def norm(at, s, third):
                squares(at, s)
                act.wait_ge(stat_done.sem, stat_done.at(at, s + 1))
                nc.scalar.activation(root[:, 0:S], stat[:, 0:S], ACT.Sqrt, bias=eps[:, 0:1]).then_inc(root_ready.sem, 1)
                high(at, third, 2)
                for d in range(DT):
                    act.wait_ge(scaled_ready.sem, scaled_ready.at(at, DT * s + d + 1))
                    nc.scalar.activation(h_high[:, d, :], work[:, d, :], ACT.Identity,
                                         bias=mod[:, d:d + 1]).then_inc(h_high_ready.sem, 1)

            act.dma_start(work_f.rearrange("p (t n) -> p t n", t=TT),
                          t["x"].rearrange("b (t p) n -> p (b t) n", p=P)).then_inc(x_landed.sem, 16)
            for i in range(3):
                act.dma_start(flat(proj[:, 16:24, :])[0:96, (2 + i) * P:(3 + i) * P],
                              t["rows_ada"][96 * i:96 * i + 96, :]).then_inc(rows_landed.sem, 16)
            act.dma_start(proj_f[0:16, P - 1:P - 1 + REL], t["rel_rows"]).then_inc(table_landed.sem, 16)
            act.dma_start(proj_f[0:32, TAB:TAB + 24], t["rel_bias_2"]).then_inc(table_landed.sem, 16)
            act.dma_start(proj_f[0:32, 2 * TAB:3 * TAB], t["one_hot"]).then_inc(table_landed.sem, 16)
            act.dma_start(proj_f[0:24, 3 * TAB:4 * TAB], t["distance_mask"]).then_inc(table_landed.sem, 16)
            act.dma_start(flat(f_bias[:, :, :]), t["forget_bias"].rearrange("l h -> (l h)").partition_broadcast(P)
                          ).then_inc(table_landed.sem, 16)
            act.wait_ge(params_ready.sem, 2)
            for i, src in ((0, CVEC), (1, CVEC), (2, CVEC + DT), (3, CVEC + DT), (4, CVEC + DT)):
                nc.scalar.activation(c_act[:, i, :], params[:, src:src + DT], ACT.Silu).then_inc(c_ready.sem, 1)
            for i in range(4):
                g = params[:, QKG + 2 * i:QKG + 2 * i + 1]
                nc.scalar.activation(g, g, ACT.Copy, scale=HEAD ** -0.5).then_inc(c_ready.sem, 1)
            act.wait_ge(table_ready.sem, 2)
            act.dma_start(table_store[0:16].rearrange("h p n -> h p n"),
                          proj_f[0:16, 0:TAB].unsqueeze(1).to_broadcast([16, P, TAB])).then_inc(table_stored.sem, 16)
            act.dma_start(table_store[16:40].rearrange("h p n -> h p n"),
                          proj_f[0:24, 4 * TAB:5 * TAB].unsqueeze(1).to_broadcast([24, P, TAB])
                          ).then_inc(table_stored.sem, 16)
            for u in range(UNITS):
                copy_ada("start", u, u % 2, mod_raw[:, 2 * u:2 * u + 2])
            act.wait_ge(table_stored.sem, 32)
            high((0, 0), 0, 0)
            high((0, 0), 1, 1)

            for b in range(2):
                with act.Fori(0, DEPTH) as l:
                    at = (b, l)

                    def ffn_act(i):
                        stage, c = 2 * i, i * (MIX + MIX_CHUNKS[b])
                        y0, q0 = TRIPS * i, i * (COLS[b] - 2 * TRIPS)

                        def silu(j, extra=None):
                            act.wait_ge(chunk_used.sem, chunk_used.at(
                                at, c + 1 + (3 * j - 1 if j else 0) , None if extra is None else extra * 6))
                            nc.scalar.activation(temp[:, 0:512], pair[0][:, :], ACT.Silu).then_inc(pair_free[0].sem, 1)

                        def hidden(j, parity, extra=None):
                            act.wait_ge(pair_free[1].sem, pair_free[1].at(
                                at, q0 // 2 + j + 1, None if extra is None else extra * 2))
                            nc.scalar.activation(flat(y_high[:, 2 * parity:2 * parity + 2, :]), temp[:, 512:1024],
                                                 ACT.Copy).then_inc(hidden_high.sem, 1)

                        norm(at, stage, c + 2)
                        silu(0)
                        hidden(0, 0)
                        with act.Fori(0, (TRIPS - 1) // 2) as r:
                            for half in range(2):
                                j = 1 + half
                                high(at, c + 3 * j, 0, r)
                                high(at, c + 3 * j + 1, 1, r)
                                copy_ada(at, 12 * stage + j - 1, (j - 1) % 2,
                                         mod_raw[:, bass.ds(r * 4 + 2 * (j - 1), 2)], r * 2)
                                silu(j, r)
                                high(at, c + 3 * j + 2, 2, r)
                                hidden(j, j % 2, r)
                        high(at, MIX if i == 0 else LAYER_CHUNKS[b], 0)
                        high(at, (MIX if i == 0 else LAYER_CHUNKS[b]) + 1, 1)
                        copy_ada(at, 12 * stage + UNITS - 2, 0, mod_raw[:, 2 * UNITS - 4:2 * UNITS - 2])
                        copy_ada(at, 12 * stage + UNITS - 1, 1, mod_raw[:, 2 * UNITS - 2:2 * UNITS])

                    def product_ready(k):
                        act.wait_ge(chunk_used.sem, chunk_used.at(at, MIX + k + 1 + 0))

                    def attention_act(first, count, chunks, load_bias, copy_gate):
                        G = GROUPS2 if b else 1
                        wide = 128 * G
                        if load_bias:
                            for i in range(2):
                                bias_load(i)
                        for i in range(count + 2):
                            if i >= 2:
                                n = first + i - 2
                                act.wait_ge(out_done.sem, out_done.at(at, n + 1))
                                tile, r0 = n // 2, HEAD * (n % 2)
                                nc.scalar.activation(y_high[r0:r0 + HEAD, tile, :], small[r0:r0 + HEAD, S:2 * S],
                                                     ACT.Copy).then_inc(y_high_ready.sem, 1)
                            if 1 <= i <= count:
                                for g in range(3):
                                    n = 3 * (first + i - 1) + g
                                    act.wait_ge(turned_done.sem, turned_done.at(at, n + 1))
                                    nc.scalar.activation(probs_t[:, 384 * g:384 * g + wide],
                                                         turned[n % 2][:, 0:wide], ACT.Copy
                                                         ).then_inc(turned_ready.sem, 1)
                            if i < count:
                                for half in range(2):
                                    n = 2 * (first + i) + half
                                    L = temp[:, 0:wide] if half == 0 else temp[:, 384:384 + 2 * wide]
                                    act.wait_ge(logits_ready.sem, logits_ready.at(at, n + 1))
                                    nc.scalar.activation(L, L, ACT.Exp, bias=neg_top[:, half:half + 1],
                                                         accum_out=total[:, half:half + 1]).then_inc(exp_ready.sem, 1)
                                if load_bias and i + 2 < count:
                                    bias_load(i + 2)
                            for k in chunks.get(i, ()):
                                high(at, MIX + k + 2, (k + 2) % 3)
                                copy_gate(k)

                    def bias_load(i):
                        src = table_groups[i] if b else table_rows[l * 8 + i]
                        dst = bias_t[:, i % 2, :]
                        dst = dst.rearrange("p (g n) -> p g n", g=3) if b else dst[:, 0:S]
                        act.dma_start(dst, src).then_inc(bias_landed[i % 2].sem, 16)

                    def unit(k):
                        u = unit_behind(b, k)
                        if u is not None:
                            copy_ada(at, 12 + u, u % 2, mod_raw[:, 2 * u:2 * u + 2])

                    def evacuate(k, q, dst, func=ACT.Copy, scale=1.0, done=None, src=None):
                        product_ready(k)
                        nc.scalar.activation(dst, pair[q % 2][:, :] if src is None else src, func, scale=scale
                                             ).then_inc((done or pair_free[q % 2]).sem, 1)

                    def out_high(bank):
                        act.wait_ge(merged_ready.sem, merged_ready.at(at, (4 if b == 0 else 0) + bank + 1))
                        nc.scalar.activation(flat(h_high[:, 2 * bank:2 * bank + 2, :]),
                                             work_f[:, 512 * bank:512 * bank + 512], ACT.Copy
                                             ).then_inc(out_high_ready.sem, 1)

                    ffn_act(0)
                    norm(at, 1, MIX + 2)
                    q = 2 * TRIPS
                    if b == 0:
                        act.dma_start(proj_f[:, 0:1536], t["pool_mats"]).then_inc(side_landed.sem, 16)
                        act.dma_start(proj_f[:, 1536:2048].rearrange("p (g e) -> p g e", g=4),
                                      t["w_pool"].rearrange("l g c e -> l c g e")[l]).then_inc(side_landed.sem, 16)
                        act.dma_start(f_raw[:, :, :], in_cols[0][l, :, :, F_LIN:F_LIN + 8]).then_inc(side_landed.sem, 16)
                        for k, (kind, a) in enumerate(MIX1):
                            if kind == "g":
                                break
                            if k > 0:
                                high(at, MIX + k + 2, (k + 2) % 3)
                            if kind == "u":
                                product_ready(k)
                                nc.scalar.activation(tok[:, :, 512 + 256 * k:768 + 256 * k],
                                                     pair[q % 2][:, :].rearrange("p (t n) -> p t n", t=2),
                                                     ACT.Copy).then_inc(pair_free[q % 2].sem, 1)
                            if kind == "gb":
                                evacuate(k, q, flat(proj[:, 16 + 2 * (k - 2):18 + 2 * (k - 2), :]),
                                         ACT.Sigmoid)
                            if kind in "qk":
                                if head_no(k) >= 1:
                                    act.wait_ge(head_stat.sem, head_stat.at(at, head_no(k)))
                                evacuate(k, q, temp[:, 0:512], ACT.Square, done=head_sq)
                            if k >= 1 and MIX1[k - 1][0] in "qk":
                                i = head_no(k - 1)
                                if i >= 1:
                                    act.wait_ge(head_rstd.sem, head_rstd.at(at, i))
                                act.wait_ge(head_stat.sem, head_stat.at(at, i + 1))
                                nc.scalar.activation(root[:, :], stat[:, :], ACT.Sqrt, bias=eps[:, 0:1]
                                                     ).then_inc(head_root.sem, 1)
                            if k == 4:
                                for g in range(4):
                                    act.wait_ge(pool_y_done.sem, pool_y_done.at(at, 1))
                                    nc.scalar.activation(y_high[:, g, :], acc[:, 512 * g + S:512 * g + 2 * S],
                                                         ACT.Copy, scale=now[:, NOW_POOL + g:NOW_POOL + g + 1]
                                                         ).then_inc(pool_high.sem, 1)
                            if k == 9:
                                act.wait_ge(side_landed.sem, side_landed.at(at, 48))
                                nc.scalar.activation(flat(f_high[:, :, :]), flat(f_raw[:, :, :]), ACT.Copy
                                                     ).then_inc(f_split.sem, 1)
                            unit(k)
                            q += kind not in ROW_KINDS
                        act.wait_ge(chain.sem, chain.at(at, 2))
                        nc.scalar.activation(flat(f_abs[:, :, :]), flat(f_abs[:, :, :]), ACT.Exp, scale=-1.0
                                             ).then_inc(step_act.sem, 1)
                        act.wait_ge(step_act.sem, step_act.at(at, 1))
                        nc.scalar.activation(flat(f_abs[:, :, :]), flat(f_abs[:, :, :]), ACT.Ln, bias=1.0
                                             ).then_inc(step_act.sem, 1)

                        def copy_gate1(k):
                            i = k - 20
                            evacuate(k, column_no(b, k), flat(proj[:, 16 + 2 * i:18 + 2 * i, :]))
                        attention_act(0, 8, {i: (20 + i // 2,) for i in range(1, 8, 2)}, True, copy_gate1)
                        attention_act(8, 8, {i: (24 + i // 2,) for i in range(1, 8, 2)}, False, copy_gate1)
                        for i in range(2):
                            g = flat(proj[:, 16 + 8 * i:24 + 8 * i, :])
                            wait_taken(act, at, b, 26)
                            wait_taken(act, at, b, 27)
                            nc.scalar.activation(g, g, ACT.Sigmoid).then_inc(gates_ready.sem, 1)
                        rest = range(28, 36)
                    else:
                        for k, (kind, a) in enumerate(MIX2):
                            if kind == "g":
                                break
                            if k > 0:
                                high(at, MIX + k + 2, (k + 2) % 3)
                            if kind == "cc":
                                if k >= 2:
                                    wait_taken(act, at, b, k - 1)
                                evacuate(k, q, temp[:, 0:512])
                            if kind == "cb":
                                i = k - 8
                                wait_taken(act, at, b, k)
                                nc.scalar.activation(flat(y_high[:, 2 * i:2 * i + 2, :]), temp[:, 512:1024], ACT.Copy
                                                     ).then_inc(conv_high.sem, 1)
                            if kind == "gc":
                                i = k - 12
                                evacuate(k, q, flat(proj[:, 24 + 2 * i:26 + 2 * i, :]), ACT.Sigmoid)
                            if kind == "q":
                                i = k - 20
                                evacuate(k, q, flat(proj[:, 2 * i:2 * i + 2, :]), scale=HEAD ** -0.5)
                            if kind == "k":
                                i = k - 26
                                evacuate(k, q, flat(proj[:, 12 + 2 * i:14 + 2 * i, :]))
                            if kind == "v":
                                i = k - 32
                                evacuate(k, q, tok[:, :, 256 * i:256 * i + 256],
                                         src=pair[q % 2][:, :].rearrange("p (t n) -> p t n", t=2))
                            unit(k)
                            q += kind not in ROW_KINDS

                        def copy_gate2(k):
                            i = k - 38
                            evacuate(k, column_no(b, k), flat(proj[:, 24 + 2 * i:26 + 2 * i, :]))
                        attention_act(0, 8, {i: (38 + i // 2,) for i in range(1, 8, 2)}, True, copy_gate2)
                        g = flat(proj[:, 24:32, :])
                        wait_taken(act, at, b, 40)
                        wait_taken(act, at, b, 41)
                        nc.scalar.activation(g, g, ACT.Sigmoid).then_inc(gates_ready.sem, 1)
                        rest = range(42, 48)
                    for k in rest:
                        high(at, MIX + k + 2, (k + 2) % 3)
                        if k == MIX_CHUNKS[b] - 5:
                            for bank in range(4):
                                out_high(bank)
                        unit(k)
                    ffn_act(1)

            squares("end", 0)
            act.wait_ge(stat_done.sem, stat_done.at("end", 1))
            nc.scalar.activation(root[:, 0:S], stat[:, 0:S], ACT.Sqrt, bias=eps[:, 0:1]).then_inc(root_ready.sem, 1)

        @block.gpsimd
        def _(pool):
            pool.memset(eps[:, :], EPS).then_inc(zeros_ready.sem, 1)
            pool.memset(zeros[:, :], 0.0).then_inc(zeros_ready.sem, 1)
            pool.wait_ge(c_ready.sem, 9)
            for b in range(2):
                with pool.Fori(0, DEPTH) as l:
                    at = (b, l)
                    copies = [(NOW_GAIN, 24, params[:, bass.ds(l * 24 + (GAIN + 48 * b), 24)]),
                              (NOW_BIAS, 72, ada_bias[:, bass.ds(l * 72 + 144 * b, 72)])]
                    if b == 0:
                        copies += [(NOW_QK, 4, params[:, bass.ds(l * 4 + QKG, 4)]),
                                   (NOW_POOL, 4, params[:, bass.ds(l * 4 + POOLS, 4)])]
                    else:
                        copies += [(NOW_CONV, 24, params[:, bass.ds(l * 24 + CONVW, 24)])]
                    pool.wait_ge(x_ready.sem, x_ready.at(at, 0))
                    for first, n, src in copies:
                        pool.tensor_copy(now[:, first:first + n], src)
                    pool.tensor_copy(now[:, NOW_C:NOW_C + DT], c_act[:, l + 2 * b, :]).then_inc(now_ready.sem, 1)
                    pool.wait_ge(x_ready.sem, x_ready.at(at, 16))
                    pool.tensor_copy(now[:, NOW_C:NOW_C + DT], c_act[:, l + 2 * b + 1, :]
                                     ).then_inc(now_ready.sem, 1)

        @block.vector
        def _(dve):
            def low(at, n, slot, extra=None):
                dve.wait_ge(w_high_ready.sem, w_high_ready.at(at, n + 1, None if extra is None else extra * 6))
                nc.vector.tensor_tensor(w_low[:, slot, :], raw[:, slot, :], w_high[:, slot, :].bitcast(F32),
                                        ALU.subtract).then_inc(w_low_ready.sem, 1)

            links = [0]

            def linked(ins, at):
                links[0] += 1
                ins.then_inc(chain.sem, 1)
                dve.wait_ge(chain.sem, chain.at(at, links[0]))

            def row_tiles_sum(w, cvec, part):
                nc.vector.tensor_scalar(w[:, 0, :], w[:, 0, :], cvec[:, 0:1], None, ALU.mult
                                        ).then_inc(ada_part.sem, 1)
                for k in range(1, DT):
                    dve.wait_ge(ada_part.sem, part(k))
                    nc.vector.scalar_tensor_tensor(out=w[:, 0, :], in0=w[:, k, :], scalar=cvec[:, k:k + 1],
                                                   in1=w[:, 0, :], op0=ALU.mult, op1=ALU.add
                                                   ).then_inc(ada_part.sem, 1)

            def ada_sum(at, u, slot, trips=None):
                step = None if trips is None else trips * 16
                dve.wait_ge(ada_landed[slot].sem, ada_landed[slot].at(at, 16 * (u // 2 + 1), step))
                row_tiles_sum(cols3(ada_raw[:, slot, :]), now[:, NOW_C:NOW_C + DT],
                              lambda k: ada_part.at(at, DT * u + k, step))

            def modulation(at, s):
                dve.wait_ge(ada_copied.sem, ada_copied.at(at, 12 * s))
                if s == 0:
                    dve.wait_ge(now_ready.sem, now_ready.at(at, 1))
                dve.wait_ge(x_ready.sem, x_ready.at(at, 8 * s))
                nc.vector.tensor_tensor(mod[:, :], mod_raw[:, :], now[:, NOW_BIAS + 24 * s:NOW_BIAS + 24 * s + 24],
                                        ALU.add).then_inc(mod_summed.sem, 1)
                dve.wait_ge(mod_summed.sem, mod_summed.at(at, s + 1))
                nc.vector.scalar_tensor_tensor(out=mod_a[:, :], in0=mod[:, 8:16], scalar=1.0,
                                               in1=now[:, NOW_GAIN + 8 * s:NOW_GAIN + 8 * s + 8],
                                               op0=ALU.add, op1=ALU.mult)
                nc.vector.tensor_scalar(mod_g[:, :], mod[:, 16:24], 1.0 if s == 1 else 0.5, None,
                                        ALU.mult).then_inc(mod_ready.sem, 1)

            def norm(at, s):
                modulation(at, s)
                dve.wait_ge(root_ready.sem, root_ready.at(at, s + 1))
                nc.vector.reciprocal(rstd[:, 0:S], root[:, 0:S]).then_inc(rstd_ready.sem, 1)
                dve.wait_ge(rstd_ready.sem, rstd_ready.at(at, s + 1))
                dve.wait_ge(mod_ready.sem, mod_ready.at(at, s + 1))

                def rest(d):
                    dve.wait_ge(h_high_ready.sem, h_high_ready.at(at, DT * s + d + 1))
                    nc.vector.scalar_tensor_tensor(out=h_low[:, d, :], in0=work[:, d, :], scalar=mod[:, d:d + 1],
                                                   in1=h_high[:, d, :].bitcast(F32), op0=ALU.add,
                                                   op1=ALU.subtract).then_inc(h_ready.sem, 1)
                for d in range(DT):
                    nc.vector.scalar_tensor_tensor(out=work[:, d, :], in0=x[:, d, :], scalar=mod_a[:, d:d + 1],
                                                   in1=rstd[:, 0:S], op0=ALU.mult, op1=ALU.mult
                                                   ).then_inc(scaled_ready.sem, 1)
                    if d >= 1:
                        rest(d - 1)
                rest(DT - 1)

            def update(at, n_last, a0):
                for d in range(DT):
                    acc_wait(at, n_last, a0, d // 2)
                    nc.vector.scalar_tensor_tensor(out=x[:, d, :], in0=acc[:, S * d:S * d + S],
                                                   scalar=mod_g[:, d:d + 1], in1=x[:, d, :],
                                                   op0=ALU.mult, op1=ALU.add).then_inc(x_ready.sem, 1)

            def acc_wait(at, n_last, a0, bank):
                if bank < 3:
                    dve.wait_ge(acc_done.sem, acc_done.at(at, 3 * a0 + bank + 1))
                else:
                    dve.wait_ge(chunk_used.sem, chunk_used.at(at, n_last + 1))

            nc.vector.memset(ones[:, :], 1.0).then_inc(zeros_ready.sem, 1)
            dve.wait_ge(params_turned.sem, 1)
            nc.vector.tensor_copy(params[:, :], pair[0][:, 0:PARAMS]).then_inc(params_ready.sem, 1)
            nc.vector.tensor_copy(ada_bias[:, :], pair[1][:, 0:4 * 72]).then_inc(params_ready.sem, 1)
            dve.wait_ge(table_landed.sem, 80)
            nc.vector.tensor_copy(proj_f[0:16, 0:P - 1], proj_f[0:16, P - 1:P].to_broadcast([16, P - 1])
                                  ).then_inc(table_ready.sem, 1)
            dve.wait_ge(params_turned.sem, 2)
            nc.vector.tensor_tensor(proj_f[0:24, 4 * TAB:5 * TAB], stat[0:24, 0:TAB],
                                    proj_f[0:24, 3 * TAB:4 * TAB], ALU.add).then_inc(table_ready.sem, 1)
            for d in range(DT):
                dve.wait_ge(x_turned.sem, 1)
                nc.vector.tensor_copy(x[:, d, :], acc[:, S * d:S * d + S]).then_inc(x_ready.sem, 1)

            dve.wait_ge(c_ready.sem, 1)
            for n, u in enumerate(FIRST_SUMMED):
                slot, landed = first_slots[u % FIRST_RING]
                dve.wait_ge(landed.sem, 16 * (u // FIRST_RING + 1))
                row_tiles_sum(cols3(slot), c_act[:, 0, :], lambda k: DT * n + k)
            low((0, 0), 0, 0)
            low((0, 0), 1, 1)

            for b in range(2):
                with dve.Fori(0, DEPTH) as l:
                    at = (b, l)
                    links[0] = 0

                    def ffn_dve(i):
                        stage, c = 2 * i, i * (MIX + MIX_CHUNKS[b])
                        y0, q0 = TRIPS * i, i * (COLS[b] - 2 * TRIPS)

                        def hidden(j, parity, extra=None):
                            e2 = None if extra is None else extra * 2
                            dve.wait_ge(pair_free[0].sem, pair_free[0].at(at, q0 // 2 + j + 1, e2))
                            dve.wait_ge(chunk_used.sem, chunk_used.at(
                                at, c + 1 + (3 * j if j else 1), None if extra is None else extra * 6))
                            nc.vector.tensor_tensor(temp[:, 512:1024], temp[:, 0:512], pair[1][:, :], ALU.mult
                                                    ).then_inc(pair_free[1].sem, 1)
                            dve.wait_ge(hidden_high.sem, hidden_high.at(at, y0 + j + 1, e2))
                            nc.vector.tensor_tensor(flat(y_low[:, 2 * parity:2 * parity + 2, :]), temp[:, 512:1024],
                                                    flat(y_high[:, 2 * parity:2 * parity + 2, :]).bitcast(F32),
                                                    ALU.subtract).then_inc(hidden_split.sem, 1)

                        norm(at, stage)
                        dve.wait_ge(now_ready.sem, now_ready.at(at, 1 + i))
                        ada_sum(at, 12 * stage, 0)
                        low(at, c + 2, 2)
                        hidden(0, 0)
                        with dve.Fori(0, (TRIPS - 1) // 2) as r:
                            for half in range(2):
                                j = 1 + half
                                low(at, c + 3 * j, 0, r)
                                low(at, c + 3 * j + 1, 1, r)
                                ada_sum(at, 12 * stage + j, j % 2, r)
                                low(at, c + 3 * j + 2, 2, r)
                                hidden(j, j % 2, r)
                        ada_sum(at, 12 * stage + UNITS - 1, 1)
                        low(at, MIX if i == 0 else LAYER_CHUNKS[b], 0)
                        low(at, (MIX if i == 0 else LAYER_CHUNKS[b]) + 1, 1)
                        update(at, c + FFN_CHUNKS - 1, 0 if i == 0 else (5 if b == 0 else 4))

                    def product_ready(k):
                        dve.wait_ge(chunk_used.sem, chunk_used.at(at, MIX + k + 1))

                    def attention_dve(first, count, chunks, forget):
                        G = GROUPS2 if b else 1
                        for i in range(count + 2):
                            if i >= 2:
                                n = first + i - 2
                                tile, r0 = n // 2, HEAD * (n % 2)
                                dve.wait_ge(y_high_ready.sem, y_high_ready.at(at, n + 1))
                                nc.vector.tensor_tensor(y_low[r0:r0 + HEAD, tile, :], small[r0:r0 + HEAD, S:2 * S],
                                                        y_high[r0:r0 + HEAD, tile, :].bitcast(F32), ALU.subtract
                                                        ).then_inc(y_ready.sem, 1)
                            if i < count:
                                m = first + i
                                if m >= 1:
                                    dve.wait_ge(turned_done.sem, turned_done.at(at, 3 * m))
                                if not forget:
                                    dve.wait_ge(bias_landed[i % 2].sem, bias_landed[i % 2].at(at, 16 * (i // 2 + 1)))
                                if b == 0 and not forget:
                                    linked(nc.vector.memset(bias_t[0:HEAD, i % 2, 192:256], NEG), at)
                                for half in range(2):
                                    w = 128 if half == 0 else 256
                                    L = temp[:, 0:G * w] if half == 0 else temp[:, 384:384 + G * w]
                                    sc = scores_a[:, 0:G * w] if half == 0 else scores_b[:, 0:G * w]
                                    dve.wait_ge(scores_done.sem, scores_done.at(at, 2 * m + half + 1))
                                    if forget:
                                        bias = causal[:, 128:256] if half == 0 else causal[:, 0:256]
                                        linked(nc.vector.scalar_tensor_tensor(
                                            out=L, in0=sc, scalar=cum_q[:, half, i:i + 1], in1=bias,
                                            op0=ALU.add, op1=ALU.add), at)
                                    else:
                                        bias = bias_t[:, i % 2, 0:G * S].rearrange("p (g n) -> p g n", g=G)
                                        if half == 0:
                                            bias = bias[:, :, 128:256]
                                        v = "p (g n) -> p g n"
                                        linked(nc.vector.tensor_tensor(L.rearrange(v, g=G), sc.rearrange(v, g=G),
                                                                       bias, ALU.add), at)
                                    nc.vector.tensor_reduce(neg_top[:, half:half + 1], L, AX_X, ALU.max,
                                                            negate=True).then_inc(logits_ready.sem, 1)
                            for k in chunks.get(i, ()):
                                low(at, MIX + k + 2, (k + 2) % 3)
                            if i < count:
                                for half in range(2):
                                    n = 2 * (first + i) + half
                                    w = 128 if half == 0 else 256
                                    L = temp[:, 0:G * w] if half == 0 else temp[:, 384:384 + G * w]
                                    dve.wait_ge(exp_ready.sem, exp_ready.at(at, n + 1))
                                    linked(nc.vector.reciprocal(share[:, half:half + 1], total[:, half:half + 1]), at)
                                    nc.vector.tensor_scalar(L, L, share[:, half:half + 1], None, ALU.mult
                                                            ).then_inc(probs_ready.sem, 1)

                    def merge(k, a0, taken, gate_tile, first):
                        if first:
                            wait_taken(dve, at, b, (4, 14)[b])
                            wait_taken(dve, at, b, (5, 15)[b])
                        else:
                            dve.wait_ge(gates_ready.sem, gates_ready.at(at, (2, 1)[b]))
                        for bank in range(4):
                            acc_wait(at, MIX + k, a0, bank)
                            w = slice(512 * bank, 512 * bank + 512)
                            g = flat(proj[:, gate_tile + 2 * bank:gate_tile + 2 * bank + 2, :])
                            if first:
                                nc.vector.tensor_tensor(work_f[:, w], acc[:, w], g, ALU.mult
                                                        ).then_inc(acc_taken.sem, 1)
                            else:
                                nc.vector.tensor_tensor(temp[:, 0:512] if bank % 2 else temp[:, 512:1024],
                                                        acc[:, w], g, ALU.mult).then_inc(acc_taken.sem, 1)
                                dve.wait_ge(acc_taken.sem, acc_taken.at(at, taken + bank + 1))
                                nc.vector.tensor_tensor(work_f[:, w], work_f[:, w],
                                                        temp[:, 0:512] if bank % 2 else temp[:, 512:1024],
                                                        ALU.add).then_inc(merged_ready.sem, 1)

                    def out_low(bank):
                        dve.wait_ge(out_high_ready.sem, out_high_ready.at(at, bank + 1))
                        nc.vector.tensor_tensor(flat(h_low[:, 2 * bank:2 * bank + 2, :]),
                                                work_f[:, 512 * bank:512 * bank + 512],
                                                flat(h_high[:, 2 * bank:2 * bank + 2, :]).bitcast(F32),
                                                ALU.subtract).then_inc(out_split.sem, 1)

                    def unit(k):
                        u = unit_behind(b, k + 2)
                        if u is not None:
                            ada_sum(at, 12 + u, u % 2)

                    ffn_dve(0)
                    norm(at, 1)
                    q = 2 * TRIPS
                    if b == 0:
                        for k, (kind, a) in enumerate(MIX1):
                            if kind == "g":
                                break
                            low(at, MIX + k + 2, (k + 2) % 3)
                            unit(k)
                            if k == 3:
                                for g in range(4):
                                    dve.wait_ge(pool_d_done.sem, pool_d_done.at(at, 1))
                                    nc.vector.tensor_copy(proj[:, 8 + g, :], acc[:, 512 * g:512 * g + S]
                                                          ).then_inc(pool_d_ready.sem, 1)
                            if k == 4:
                                for g in range(4):
                                    dve.wait_ge(pool_high.sem, pool_high.at(at, g + 1))
                                    nc.vector.scalar_tensor_tensor(
                                        out=y_low[:, g, :], in0=acc[:, 512 * g + S:512 * g + 2 * S],
                                        scalar=now[:, NOW_POOL + g:NOW_POOL + g + 1],
                                        in1=y_high[:, g, :].bitcast(F32), op0=ALU.mult, op1=ALU.subtract
                                    ).then_inc(pool_ready.sem, 1)
                            if k == 7:
                                merge(7, 1, 0, 16, True)
                            if kind in "qk":
                                i = head_no(k)
                                dve.wait_ge(head_sq.sem, head_sq.at(at, i + 1))
                                nc.vector.tensor_copy(flat(proj[:, 2 * i:2 * i + 2, :]), pair[q % 2][:, :]
                                                      ).then_inc(pair_free[q % 2].sem, 1)
                            if kind == "v":
                                i = k - 12 if k < 14 else k - 18 + 4
                                product_ready(k)
                                nc.vector.tensor_copy(tok[:, :, 256 * i:256 * i + 256],
                                                      pair[q % 2][:, :].rearrange("p (t n) -> p t n", t=2)
                                                      ).then_inc(pair_free[q % 2].sem, 1)
                            if k >= 1 and MIX1[k - 1][0] in "qk":
                                i = head_no(k - 1)
                                w = flat(proj[:, 2 * i:2 * i + 2, :])
                                kind_of = (0, 0, 1, 1, 2, 2, 3, 3)[i]
                                if i >= 1:
                                    dve.wait_ge(head_normed.sem, head_normed.at(at, i))
                                dve.wait_ge(head_root.sem, head_root.at(at, i + 1))
                                nc.vector.reciprocal(rstd[:, :], root[:, :]).then_inc(head_rstd.sem, 1)
                                dve.wait_ge(head_rstd.sem, head_rstd.at(at, i + 1))
                                nc.vector.scalar_tensor_tensor(
                                    out=w, in0=w, scalar=now[:, NOW_QK + kind_of:NOW_QK + kind_of + 1],
                                    in1=rstd[:, :], op0=ALU.mult, op1=ALU.mult).then_inc(head_normed.sem, 1)
                            if k == 9:
                                dve.wait_ge(f_split.sem, f_split.at(at, 1))
                                nc.vector.tensor_tensor(flat(f_low[:, :, :]), flat(f_raw[:, :, :]),
                                                        flat(f_high[:, :, :]).bitcast(F32), ALU.subtract
                                                        ).then_inc(f_split.sem, 1)
                            q += kind not in ROW_KINDS
                        dve.wait_ge(f_done.sem, f_done.at(at, 1))
                        linked(nc.vector.tensor_tensor(f_val[:, :, :], small[:, 16:32].rearrange("p (t h) -> p t h", t=TT),
                                                       f_bias[:, l, :].unsqueeze(1).to_broadcast([P, TT, 8]),
                                                       ALU.add), at)
                        linked(nc.vector.scalar_tensor_tensor(
                            out=flat(f_abs[:, :, :]), in0=flat(f_val[:, :, :]), scalar=-1.0,
                            in1=flat(f_val[:, :, :]), op0=ALU.mult, op1=ALU.max), at)
                        dve.wait_ge(step_act.sem, step_act.at(at, 2))
                        nc.vector.scalar_tensor_tensor(
                            out=flat(logf[:, :, :]), in0=flat(f_val[:, :, :]), scalar=0.0,
                            in1=flat(f_abs[:, :, :]), op0=ALU.min, op1=ALU.subtract).then_inc(f_ready.sem, 1)
                        attention_dve(0, 8, {i: (20 + i // 2,) for i in range(1, 8, 2)}, False)
                        dve.wait_ge(cum_done.sem, cum_done.at(at, 2))
                        nc.vector.tensor_copy(flat(cum_q[:, :, :]), small[:, 32:48]).then_inc(cum_ready.sem, 1)
                        nc.vector.tensor_scalar(cum_k, small[0:8, S:2 * S], -1.0, None, ALU.mult
                                                ).then_inc(cum_ready.sem, 1)
                        dve.wait_ge(cum_ready.sem, cum_ready.at(at, 2))
                        attention_dve(8, 8, {i: (24 + i // 2,) for i in range(1, 8, 2)}, True)
                        unit(27)
                        low(at, MIX + 30, 0)
                        low(at, MIX + 31, 1)
                        unit(29)
                        merge(29, 2, 4, 16, False)
                        low(at, MIX + 32, 2)
                        low(at, MIX + 33, 0)
                        unit(31)
                        merge(31, 3, 8, 24, False)
                        first_out, a_out = 32, 4
                    else:
                        nc.vector.memset(conv_u()[:, :, 0:2], 0.0)
                        for k, (kind, a) in enumerate(MIX2):
                            if kind == "g":
                                break
                            low(at, MIX + k + 2, (k + 2) % 3)
                            unit(k)
                            if kind == "ch":
                                i = k // 2
                                wait_taken(dve, at, b, k - 1)
                                product_ready(k)
                                nc.vector.tensor_tensor(conv_u()[:, 2 * i:2 * i + 2, 2:2 + S],
                                                        temp[:, 0:512].rearrange("p (a n) -> p a n", a=2),
                                                        pair[q % 2][:, :].rearrange("p (a n) -> p a n", a=2),
                                                        ALU.mult).then_inc(pair_free[q % 2].sem, 1)
                            if kind == "cb":
                                i = k - 8
                                wait_taken(dve, at, b, 7)
                                if i >= 1:
                                    dve.wait_ge(conv_split.sem, conv_split.at(at, i))
                                for tap in range(3):
                                    for a2 in range(2):
                                        d = 2 * i + a2
                                        dst = temp[:, S * a2:S * a2 + S]
                                        u = conv_u()[:, d, tap:tap + S]
                                        w = now[:, NOW_CONV + 8 * tap + d:NOW_CONV + 8 * tap + d + 1]
                                        if tap == 0:
                                            ins = nc.vector.tensor_scalar(dst, u, w, None, ALU.mult)
                                        else:
                                            ins = nc.vector.scalar_tensor_tensor(out=dst, in0=u, scalar=w, in1=dst,
                                                                                 op0=ALU.mult, op1=ALU.add)
                                    if tap < 2:
                                        linked(ins, at)
                                ins.then_inc(conv_ready.sem, 1)
                                dve.wait_ge(conv_ready.sem, conv_ready.at(at, i + 1))
                                product_ready(k)
                                nc.vector.tensor_tensor(temp[:, 512:1024], temp[:, 0:512], pair[q % 2][:, :],
                                                        ALU.mult).then_inc(pair_free[q % 2].sem, 1)
                                dve.wait_ge(conv_high.sem, conv_high.at(at, i + 1))
                                nc.vector.tensor_tensor(flat(y_low[:, 2 * i:2 * i + 2, :]), temp[:, 512:1024],
                                                        flat(y_high[:, 2 * i:2 * i + 2, :]).bitcast(F32),
                                                        ALU.subtract).then_inc(conv_split.sem, 1)
                            if k == 19:
                                merge(19, 1, 0, 24, True)
                            q += kind not in ROW_KINDS
                        attention_dve(0, 8, {i: (38 + i // 2,) for i in range(1, 8, 2)}, False)
                        low(at, MIX + 44, 2)
                        low(at, MIX + 45, 0)
                        merge(43, 2, 4, 24, False)
                        first_out, a_out = 44, 3
                    for bank in range(4):
                        out_low(bank)
                    for k in range(first_out, first_out + 4):
                        low(at, MIX + k + 2, (k + 2) % 3)
                    update(at, MIX + MIX_CHUNKS[b] - 1, a_out)
                    assert links[0] == chain.per[b], links
                    ffn_dve(1)

            dve.wait_ge(root_ready.sem, root_ready.at("end", 1))
            nc.vector.reciprocal(rstd[:, 0:S], root[:, 0:S]).then_inc(rstd_ready.sem, 1)
            dve.wait_ge(rstd_ready.sem, rstd_ready.at("end", 1))
            for d in range(DT):
                nc.vector.scalar_tensor_tensor(out=work[:, d, :], in0=x[:, d, :],
                                               scalar=params[:, GAIN + 96 + d:GAIN + 97 + d],
                                               in1=rstd[:, 0:S], op0=ALU.mult, op1=ALU.mult
                                               ).then_inc(scaled_ready.sem, 1)
            dve.wait_ge(result_turned.sem, 1)
            for bank in range(4):
                nc.vector.tensor_copy(proj_f[:, 512 * bank:512 * bank + 512], acc[:, 512 * bank:512 * bank + 512]
                                      ).then_inc(result_ready.sem, 1)

        @block.tensor
        def _(pe):
            mm = nc.tensor.matmul

            def triple(dst, a_h, a_l, b_h, b_l, start):
                mm(dst, a_h, b_h, start=start, stop=False, skip_group_check=True)
                mm(dst, a_h, b_l, start=False, stop=False, skip_group_check=True)
                return mm(dst, a_l, b_h, start=False, stop=True, skip_group_check=True)

            def column(at, n, q, slot, token_major=False, stage=None, extra=None, q_extra=None):
                pe.wait_ge(w_low_ready.sem, w_low_ready.at(at, n + 1, extra))
                free = pair_free[q % 2]
                pe.wait_ge(free.sem, free.at(at, q // 2, q_extra))
                wh, wl = cols3(w_high[:, slot, :]), cols3(w_low[:, slot, :])
                for k in range(DT):
                    if stage is not None:
                        pe.wait_ge(h_ready.sem, h_ready.at(at, DT * stage + k + 1))
                    for i in range(2):
                        dst = pair[q % 2][:, S * i:S * i + S]
                        c = slice(P * i, P * i + P)
                        if token_major:
                            last = triple(dst, h_high[:, k, c], h_low[:, k, c], wh[:, k, :], wl[:, k, :],
                                          k == 0 and i == 0)
                        else:
                            last = triple(dst, wh[:, k, c], wl[:, k, c], h_high[:, k, :], h_low[:, k, :],
                                          k == 0 and i == 0)
                last.then_inc(chunk_used.sem, 1)

            def row(at, n, slot, src_h, src_l, tiles, start=False, last=False, extra=None, banks=None):
                pe.wait_ge(w_low_ready.sem, w_low_ready.at(at, n + 1, extra))
                wh, wl = rows3(w_high[:, slot, :]), rows3(w_low[:, slot, :])
                for d in range(DT):
                    for kk in range(2):
                        if banks is not None and kk == 0 and d % 2 == 0:
                            pe.wait_ge(acc_taken.sem, acc_taken.at(at, banks + d // 2 + 1))
                        c = slice(P * d, P * d + P)
                        ins = triple(acc[:, S * d:S * d + S], wh[:, kk, c], wl[:, kk, c],
                                     src_h[:, tiles[kk], :], src_l[:, tiles[kk], :],
                                     start and kk == 0 and d % 2 == 0)
                        if last and kk == 1 and d % 2 == 1 and d < DT - 1:
                            ins.then_inc(acc_done.sem, 1)
                ins.then_inc(chunk_used.sem, 1)

            def clear_acc():
                for bank in [*range(4)] * 2:
                    mm(acc[:, 512 * bank:512 * bank + 512], zeros[0:1, 0:P], zeros[0:1, :], start=True,
                       stop=True, skip_group_check=True)

            def first_ada(u):
                slot, landed = first_slots[u % FIRST_RING]
                pe.wait_ge(ada_copied.sem, u + 2)
                w = cols3(slot)
                if u in FIRST_SUMMED:
                    pe.wait_ge(ada_part.sem, DT * (FIRST_SUMMED.index(u) + 1))
                    tiles = [(0, ones[:, :])]
                else:
                    pe.wait_ge(landed.sem, 16 * (u // FIRST_RING + 1))
                    tiles = [(k, c_act[:, 0, k:k + 1]) for k in range(DT)]
                for i in range(2):
                    for k, factor in tiles:
                        last = mm(small[:, 2 * (u % 2) + i:2 * (u % 2) + i + 1], w[:, k, P * i:P * i + P], factor,
                                  start=k == 0, stop=k == tiles[-1][0], skip_group_check=True)
                last.then_inc(ada_used.sem, 1)

            def ada(at, u, slot, part_extra=None, extra=None):
                pe.wait_ge(ada_part.sem, ada_part.at(at, DT * (u + 1), part_extra))
                pe.wait_ge(ada_copied.sem, ada_copied.at(at, u, extra))
                for i in range(2):
                    last = mm(small[:, 2 * slot + i:2 * slot + i + 1], ada_raw[:, slot, P * i:P * i + P],
                              ones[:, :], start=True, stop=True, skip_group_check=True)
                last.then_inc(ada_used.sem, 1)

            def mean_square(at, s):
                for d in range(DT):
                    pe.wait_ge(squares_ready.sem, squares_ready.at(at, DT * s + d + 1))
                    last = mm(stat[:, 0:S], mean_all, work[:, d, :], start=d == 0, stop=d == DT - 1)
                last.then_inc(stat_done.sem, 1)

            pe.sem_inc(chunk_used.sem, 3)
            pe.sem_inc(w_low_ready.sem, 3)
            pe.sem_inc(ada_used.sem, 2)
            pe.sem_inc(ada_copied.sem, 2)
            for free in pair_free:
                pe.sem_inc(free.sem, 1)
            pe.wait_ge(const_landed.sem, 16)
            pe.wait_ge(rows_landed.sem, 80)
            stage_rows = flat(proj[:, 16:24, :])
            nc.tensor.transpose(pair[0][:, 0:120], stage_rows[0:120, 0:P], ident[0:120, 0:120])
            nc.tensor.transpose(pair[0][:, 120:184], stage_rows[0:64, P:2 * P], ident[0:64, 0:64])
            for i in range(3):
                last = nc.tensor.transpose(pair[1][:, 96 * i:96 * i + 96], stage_rows[0:96, (2 + i) * P:(3 + i) * P],
                                           ident[0:96, 0:96])
            last.then_inc(params_turned.sem, 1)
            pe.wait_ge(table_landed.sem, 80)
            mm(stat[0:24, 0:TAB], proj_f[0:32, TAB:TAB + 24], proj_f[0:32, 2 * TAB:3 * TAB], start=True,
               stop=True).then_inc(params_turned.sem, 1)
            pe.wait_ge(x_landed.sem, 16)
            for d in range(DT):
                for tt in range(TT):
                    last = nc.tensor.transpose(acc[:, S * d + P * tt:S * d + P * tt + P],
                                               work_f[:, D * tt + P * d:D * tt + P * d + P], ident)
            last.then_inc(x_turned.sem, 1)
            pe.wait_ge(c_ready.sem, 5)
            pe.wait_ge(zeros_ready.sem, 3)
            for u in range(UNITS):
                first_ada(u)

            for b in range(2):
                with pe.Fori(0, DEPTH) as l:
                    at = (b, l)

                    def ffn_pe(i):
                        stage, c = 2 * i, i * (MIX + MIX_CHUNKS[b])
                        q0 = i * (COLS[b] - 2 * TRIPS)
                        y0 = 11 * i
                        mean_square(at, stage)
                        clear_acc()
                        column(at, c, q0, 0, stage=stage)
                        column(at, c + 1, q0 + 1, 1)
                        ada(at, 12 * stage, 0)
                        with pe.Fori(0, (TRIPS - 1) // 2) as r:
                            for half in range(2):
                                j = 1 + half
                                column(at, c + 3 * j - 1, q0 + 2 * j, 2, extra=r * 6, q_extra=r * 2)
                                column(at, c + 3 * j, q0 + 2 * j + 1, 0, extra=r * 6, q_extra=r * 2)
                                pe.wait_ge(hidden_split.sem, hidden_split.at(at, y0 + j, r * 2))
                                e = 2 * ((j - 1) % 2)
                                row(at, c + 3 * j + 1, 1, y_high, y_low, (e, e + 1), extra=r * 6)
                                ada(at, 12 * stage + j, j % 2, r * 16, r * 2)
                        pe.wait_ge(hidden_split.sem, hidden_split.at(at, y0 + TRIPS))
                        row(at, c + FFN_CHUNKS - 1, 2, y_high, y_low, (0, 1), last=True)
                        ada(at, 12 * stage + UNITS - 1, 1)

                    def head_ops(first, forget):
                        G = GROUPS2 if b else 1
                        v = "p (g n) -> p g n"

                        def qk(m, g):
                            h = m - first
                            r0 = HEAD * (h % 2)
                            if b:
                                qt, kt = 4 * g + h // 2, 12 + 4 * g + h // 2
                            else:
                                qt, kt = (8 if forget else 0) + h // 2, (12 if forget else 4) + h // 2
                            return proj[r0:r0 + HEAD, qt, :], proj[r0:r0 + HEAD, kt, :]

                        def scores(m):
                            if m >= 1:
                                pe.wait_ge(logits_ready.sem, logits_ready.at(at, 2 * m))
                            for half in range(2):
                                w = 128 * (1 + half)
                                dst = scores_b if half else scores_a
                                for g in range(G):
                                    qq, kk = qk(m, g)
                                    last = mm(dst[:, w * g:w * g + w], qq[:, P * half:P * half + P], kk[:, 0:w],
                                              start=True, stop=not forget, skip_group_check=True)
                                if forget:
                                    h = m - first
                                    last = mm(dst[:, 0:w], ident[0:8, h:h + 1].to_broadcast([8, P]), cum_k[:, 0:w],
                                              start=False, stop=True, skip_group_check=True)
                                last.then_inc(scores_done.sem, 1)

                        def turn(m):
                            for g3 in range(3):
                                n = 3 * m + g3
                                half = 0 if g3 == 0 else 1
                                if g3 < 2:
                                    pe.wait_ge(probs_ready.sem, probs_ready.at(at, 2 * m + half + 1))
                                if n >= 2:
                                    pe.wait_ge(turned_ready.sem, turned_ready.at(at, n - 1))
                                for g in range(G):
                                    o = P * g if g3 == 0 else 384 + S * g + P * (g3 - 1)
                                    last = nc.tensor.transpose(turned[n % 2][:, P * g:P * g + P],
                                                               temp[:, o:o + P], ident)
                                last.then_inc(turned_done.sem, 1)

                        def values(m):
                            h = m - first
                            pe.wait_ge(ada_copied.sem, ada_copied.at(at, 12 + UNITS - (3, 0)[b]))
                            if m >= 1:
                                pe.wait_ge(y_ready.sem, y_ready.at(at, m))
                            pe.wait_ge(turned_ready.sem, turned_ready.at(at, 3 * m + 3))
                            base = 0 if not forget else 1024
                            for half in range(2):
                                parts = [(0, 0)] if half == 0 else [(0, 1), (1, 2)]
                                todo = [(g, kt, g3) for kt, g3 in parts for g in range(G)]
                                for j, (g, kt, g3) in enumerate(todo):
                                    c = (512 * g if b else base) + P * (h // 2)
                                    last = mm(small[:, S + P * half:S + P * half + P], tok[:, kt, c:c + P],
                                              probs_t[:, 384 * g3 + P * g:384 * g3 + P * g + P],
                                              start=j == 0, stop=j == len(todo) - 1, skip_group_check=True)
                            last.then_inc(out_done.sem, 1)
                        return scores, turn, values

                    def attention_pe(first, count, chunks, forget, q_first):
                        scores, turn, values = head_ops(first, forget)
                        for i in range(count + 2):
                            if i < count:
                                scores(first + i)
                            if i >= 2:
                                values(first + i - 2)
                            if 1 <= i <= count:
                                turn(first + i - 1)
                            for k in chunks.get(i, ()):
                                column(at, MIX + k, q_first + k - chunks[1][0], k % 3)

                    def unit(k):
                        u = unit_behind(b, k)
                        if u is not None:
                            ada(at, 12 + u, u % 2)

                    ffn_pe(0)
                    mean_square(at, 1)
                    q = 2 * TRIPS
                    if b == 0:
                        for k, (kind, a) in enumerate(MIX1):
                            if kind == "g":
                                break
                            if kind == "wb":
                                if k == 6:
                                    pe.wait_ge(pool_ready.sem, pool_ready.at(at, 4))
                                i = k - 6
                                row(at, MIX + k, k % 3, y_high, y_low, (2 * i, 2 * i + 1), start=i == 0, last=i == 1)
                            else:
                                column(at, MIX + k, q, k % 3, kind in TOKEN_KINDS, 1 if k == 0 else None)
                                q += 1
                            if k == 2:
                                wait_taken(pe, at, b, 0)
                                wait_taken(pe, at, b, 1)
                                pe.wait_ge(side_landed.sem, side_landed.at(at, 48))
                                for g in range(4):
                                    mm(acc[:, 512 * g:512 * g + S], tok[:, 0, 512 + P * g:512 + P * g + P],
                                       proj_f[:, 384 * g:384 * g + S], start=True, stop=False, skip_group_check=True)
                                    last = mm(acc[:, 512 * g + P:512 * g + S], tok[:, 1, 512 + P * g:512 + P * g + P],
                                              proj_f[:, 384 * g + S:384 * g + S + P], start=False, stop=True,
                                              skip_group_check=True)
                                last.then_inc(pool_d_done.sem, 1)
                            if k == 3:
                                for g in range(4):
                                    pe.wait_ge(pool_d_ready.sem, pool_d_ready.at(at, g + 1))
                                    last = mm(acc[:, 512 * g + S:512 * g + 2 * S], proj_f[:, 1536 + P * g:1536 + P * g + P],
                                              proj[:, 8 + g, :], start=True, stop=True, skip_group_check=True)
                                last.then_inc(pool_y_done.sem, 1)
                            if k >= 1 and MIX1[k - 1][0] in "qk":
                                i = head_no(k - 1)
                                pe.wait_ge(head_sq.sem, head_sq.at(at, i + 1))
                                if i >= 1:
                                    pe.wait_ge(head_root.sem, head_root.at(at, i))
                                mm(stat[:, :], mean_head, temp[:, 0:512], start=True, stop=True
                                   ).then_inc(head_stat.sem, 1)
                            unit(k)
                        pe.wait_ge(f_split.sem, f_split.at(at, 2))
                        pe.wait_ge(ada_copied.sem, ada_copied.at(at, 12 + 9))
                        for tt in range(TT):
                            for k in range(DT):
                                c = slice(P * tt, P * tt + P)
                                last = triple(small[:, 16 + 8 * tt:24 + 8 * tt], h_high[:, k, c], h_low[:, k, c],
                                              f_high[:, k, :], f_low[:, k, :], tt == 0 and k == 0)
                        last.then_inc(f_done.sem, 1)
                        pe.wait_ge(head_normed.sem, head_normed.at(at, 8))
                        wait_taken(pe, at, b, 18)
                        wait_taken(pe, at, b, 19)
                        attention_pe(0, 8, {i: (20 + i // 2,) for i in range(1, 8, 2)}, False, q)
                        pe.wait_ge(f_ready.sem, f_ready.at(at, 1))
                        pe.wait_ge(y_ready.sem, y_ready.at(at, 8))
                        mm(small[:, 32:40], upto[:, 0:P], logf[:, 0, :], start=True, stop=True, skip_group_check=True)
                        mm(small[:, 40:48], upto[:, P:S], logf[:, 0, :], start=True, stop=False, skip_group_check=True)
                        mm(small[:, 40:48], upto[:, 0:P], logf[:, 1, :], start=False, stop=True,
                           skip_group_check=True).then_inc(cum_done.sem, 1)
                        mm(small[0:8, S:2 * S], logf[:, 0, :], upto, start=True, stop=False, skip_group_check=True)
                        mm(small[0:8, S + P:2 * S], logf[:, 1, :], upto[:, 0:P], start=False, stop=True,
                           skip_group_check=True).then_inc(cum_done.sem, 1)
                        pe.wait_ge(cum_ready.sem, cum_ready.at(at, 2))
                        attention_pe(8, 8, {i: (24 + i // 2,) for i in range(1, 8, 2)}, True, q + 4)
                        pe.wait_ge(y_ready.sem, y_ready.at(at, 16))
                        for i in range(2):
                            row(at, MIX + 28 + i, (28 + i) % 3, y_high, y_low, (2 * i, 2 * i + 1),
                                start=i == 0, last=i == 1)
                            unit(28 + i)
                        for i in range(2):
                            row(at, MIX + 30 + i, (30 + i) % 3, y_high, y_low, (4 + 2 * i, 5 + 2 * i),
                                start=i == 0, last=i == 1, banks=4 if i == 0 else None)
                            unit(30 + i)
                        first_out, taken = 32, 8
                    else:
                        for k, (kind, a) in enumerate(MIX2):
                            if kind == "g":
                                break
                            if kind == "wconv":
                                i = k - 16
                                if i == 0:
                                    pe.wait_ge(conv_split.sem, conv_split.at(at, 4))
                                row(at, MIX + k, k % 3, y_high, y_low, (2 * i, 2 * i + 1), start=i == 0, last=i == 3)
                            else:
                                column(at, MIX + k, q, k % 3, kind in TOKEN_KINDS, 1 if k == 0 else None)
                                q += 1
                            unit(k)
                        wait_taken(pe, at, b, 36)
                        wait_taken(pe, at, b, 37)
                        pe.wait_ge(acc_taken.sem, acc_taken.at(at, 4))
                        attention_pe(0, 8, {i: (38 + i // 2,) for i in range(1, 8, 2)}, False, q)
                        pe.wait_ge(y_ready.sem, y_ready.at(at, 8))
                        for i in range(2):
                            row(at, MIX + 42 + i, (42 + i) % 3, y_high, y_low, (2 * i, 2 * i + 1),
                                start=i == 0, last=i == 1)
                            unit(42 + i)
                        first_out, taken = 44, 4
                    for i in range(4):
                        pe.wait_ge(out_split.sem, out_split.at(at, i + 1))
                        row(at, MIX + first_out + i, (first_out + i) % 3, h_high, h_low, (2 * i, 2 * i + 1),
                            start=i == 0, last=i == 3, banks=taken if i == 0 else None)
                        unit(first_out + i)
                    ffn_pe(1)

            mean_square("end", 0)
            for d in range(DT):
                pe.wait_ge(scaled_ready.sem, scaled_ready.at("end", d + 1))
                for tt in range(TT):
                    last = nc.tensor.transpose(acc[:, D * tt + P * d:D * tt + P * d + P],
                                               work[:, d, P * tt:P * tt + P], ident)
            last.then_inc(result_turned.sem, 1)


def constants():
    const = np.zeros((P, CONSTS), np.float32)
    const[:, ID:ID + P] = np.eye(P)
    const[:, ONES:ONES + P] = 1.0 / D
    half = np.arange(P) // HEAD
    const[:, BLOCK:BLOCK + P] = (half[:, None] == half[None, :]) / HEAD
    const[:, UPTO:UPTO + S] = np.arange(P)[:, None] <= np.arange(S)[None, :]
    const[:, CAUSAL + P:CAUSAL + S] = np.where(np.arange(P)[None, :] > np.arange(P)[:, None], NEG, 0.0)

    token = np.arange(S)
    pool = np.zeros((P, 4, 384), np.float32)
    for g, w in enumerate(POOL_W):
        back = token[None, :] - token[:, None]
        m = ((back >= 0) & (back < w)) / np.minimum(token + 1, w)[None, :] - (back == 0)
        pool[:, g, 0:S] = m[0:P, :]
        pool[:, g, S:384] = m[P:S, P:S]

    exact = 16
    dist = 255 - np.arange(TAB)
    far = np.maximum(dist, 1).astype(np.float32)
    large = exact + (np.log(far / exact) / np.log(2048 / exact) * (32 - exact)).astype(np.int32)
    bucket = np.where(dist < exact, np.maximum(dist, 0), np.minimum(large, 31)).astype(np.int32)
    one_hot = np.zeros((32, TAB), np.float32)
    mask = np.full((24, TAB), NEG, np.float32)
    for g, (window, step) in enumerate(((128, 1), (512, 4), (2048, 16))):
        seen = (dist >= 0) & (dist % step == 0) & (dist <= window)
        mask[8 * g:8 * g + 8, seen] = 0.0
    one_hot[bucket[dist >= 0], np.arange(TAB)[dist >= 0]] = 1.0
    return const, pool.reshape(P, 1536), one_hot, mask


def kernel(**inputs):
    import concourse.bacc as _bacc
    from concourse.bass_utils import run_bass_kernel_spmd as _run

    a = {k: np.asarray(v) for k, v in inputs.items()}
    row = lambda *parts: np.concatenate([np.ascontiguousarray(p).reshape(-1, P) for p in parts])
    const, pool, one_hot, mask = constants()
    gains = np.repeat(a["qk_gain"].reshape(8, 1, HEAD), 2, axis=1)
    arrays = {
        "x": a["x"],
        "w_ada_all": np.concatenate([a["w_ada"], a["ada_w_2"]]),
        "ffn_gate_all": np.concatenate([a["ffn_w_gate"], a["ffn_w_gate_2"]]),
        "ffn_up_all": np.concatenate([a["ffn_w_up"], a["ffn_w_up_2"]]),
        "ffn_down_all": np.concatenate([a["ffn_w_down"], a["ffn_w_down_2"]]),
        "w_in": a["w_in"], "w_in_2": a["w_in_2"], "w_branch": a["w_branch"], "w_out": a["w_out"],
        "w_pool": a["w_pool"], "forget_bias": a["forget_bias"], "rel_bias_2": a["rel_bias_2"],
        "w_conv_out_2": a["w_conv_out_2"], "w_attn_out_2": a["w_attn_out_2"], "w_o_2": a["w_o_2"],
        "rel_rows": np.ascontiguousarray(a["rel_bias"].reshape(16, REL)[:, ::-1]),
        "rows_a": row(a["norm_gain"], a["norm_g_2"], a["final_g_2"], gains, a["pool_scale"]),
        "rows_b": row(a["conv_w_2"], a["c"], a["c_2"]),
        "rows_ada": row(a["b_ada"], a["ada_b_2"]),
        "const": const, "pool_mats": pool, "one_hot": one_hot, "distance_mask": mask,
    }
    nc = _bacc.Bacc("TRN2", target_bir_lowering=False, num_devices=1)
    tensors = {n: nc.dram_tensor(f"in_{n}", v.shape, F32, kind="ExternalInput").ap() for n, v in arrays.items()}
    out = nc.dram_tensor("out_0", (1, S, D), F32, kind="ExternalOutput").ap()
    build(nc, tensors, out)
    r = _run(nc, [{f"in_{n}": v for n, v in arrays.items()}], core_ids=[0])
    return r.results[0]["out_0"]
```

```python
from contextlib import ExitStack

import numpy as np

import concourse.bass as bass
from concourse import mybir

F32 = mybir.dt.float32
F32R = mybir.dt.float32r
BF16 = mybir.dt.bfloat16
ALU = mybir.AluOpType
ACT = mybir.ActivationFunctionType
AX_X = mybir.AxisListType.X

P = 128
D = 1024
DT = D // P
S = 256
TT = S // P
DEPTH = 2
D_FF = 2816
TRIPS = D_FF // 256
HEAD = 64
GROUPS2 = 3
REL = 257
TAB = 384
EPS = 1e-6
NEG = -1e30
POOL_W = (2, 4, 8, 16)

FFN_CHUNKS = 3 * TRIPS
MIX = FFN_CHUNKS
MIX_CHUNKS = (36, 48)
LAYER_CHUNKS = tuple(2 * FFN_CHUNKS + m for m in MIX_CHUNKS)
COLS = (2 * 2 * TRIPS + 26, 2 * 2 * TRIPS + 38)
UNITS = 12
FIRST_SUMMED = (0, 1, 2, 4, 5, 6, 8, 9, 11)
FIRST_RING = 5
HEADS = (16, 8)
TURNS = (1, 3)
TURN_STEP, VALUE_STEP = (2, 1), (3, 2)
GATES_FROM = (20, 38)

A_Q, A_K, A_V, B_U, C_Q, C_K, C_V, F_LIN, G_LIN = 0, 512, 1024, 1536, 2048, 2560, 3072, 3584, 3592
MIX1 = ([("u", B_U + 256 * i) for i in range(2)] + [("gb", G_LIN + D + 256 * i) for i in range(4)]
        + [("wb", i) for i in range(2)]
        + [("q", A_Q + 256 * i) for i in range(2)] + [("k", A_K + 256 * i) for i in range(2)]
        + [("v", A_V + 256 * i) for i in range(2)]
        + [("q", C_Q + 256 * i) for i in range(2)] + [("k", C_K + 256 * i) for i in range(2)]
        + [("v", C_V + 256 * i) for i in range(2)]
        + [("g", G_LIN + 256 * i) for i in range(4)] + [("g", G_LIN + 2 * D + 256 * i) for i in range(4)]
        + [("wa", i) for i in range(2)] + [("wc", i) for i in range(2)] + [("wo", i) for i in range(4)])
QKV2 = 1536
CONV2 = 3 * QKV2
MIX2 = ([(n, CONV2 + o + 256 * i) for i in range(4) for n, o in (("cc", D), ("ch", 2 * D))]
        + [("cb", CONV2 + 256 * i) for i in range(4)] + [("gc", CONV2 + 3 * D + 256 * i) for i in range(4)]
        + [("wconv", i) for i in range(4)]
        + [("q", 256 * i) for i in range(6)] + [("k", QKV2 + 256 * i) for i in range(6)]
        + [("v", 2 * QKV2 + 256 * i) for i in range(6)]
        + [("g", CONV2 + 4 * D + 256 * i) for i in range(4)]
        + [("wattn", i) for i in range(2)] + [("wo", i) for i in range(4)])
MIXES = (MIX1, MIX2)
ROW_KINDS = ("wb", "wa", "wc", "wo", "wconv", "wattn")
TOKEN_KINDS = ("u", "v")
assert all(len(m) == c for m, c in zip(MIXES, MIX_CHUNKS))


def column_no(b, k):
    return 2 * TRIPS + sum(kind not in ROW_KINDS for kind, _ in MIXES[b][:k])


def head_no(k):
    return k - 8 if k < 12 else k - 10


UNIT_BEHIND = ((3, 5, 7, 9, 11, 13, 15, 17, 19, 29, 34, 35), (2, 5, 8, 14, 16, 19, 22, 25, 28, 31, 34, 37))


def unit_behind(b, k):
    return UNIT_BEHIND[b].index(k) if k in UNIT_BEHIND[b] else None


GAIN, QKG, POOLS, CONVW, CVEC = 0, 104, 112, 120, 168
PARAMS = 184
NOW_GAIN, NOW_BIAS, NOW_QK, NOW_POOL, NOW_CONV, NOW_C, NOW = 0, 24, 96, 100, 104, 128, 136
ID, ONES, BLOCK, UPTO, CAUSAL, CONSTS = 0, 128, 256, 288, 544, 800


class Signal:

    def __init__(self, sem, per, start=0):
        self.sem, self.start, self.per = sem, start, per

    def at(self, where, k, extra=None):
        if where == "start":
            return k
        if where == "end":
            return self.start + DEPTH * sum(self.per) + k
        b, l = where
        value = l * self.per[b] + (self.start + (DEPTH * self.per[0] if b else 0) + k)
        return value if extra is None else value + extra


def build(nc, t, out):
    ctx = ExitStack()
    with ctx:
        def sb(name, shape, dt=F32):
            return ctx.enter_context(nc.sbuf_tensor(name, shape, dt))

        def ps(name, shape):
            return ctx.enter_context(nc.psum_tensor(name, shape, F32))

        def signal(name, per, start=0):
            return Signal(ctx.enter_context(nc.semaphore(name)), per, start)

        x = sb("x", [P, DT, S])
        h_high = sb("h_high", [P, DT, S], F32R)
        h_low = sb("h_low", [P, DT, S], F32R)
        work = sb("work", [P, DT, S])
        raw = sb("raw", [P, 3, 2048])
        w_high = sb("w_high", [P, 3, 2048], F32R)
        w_low = sb("w_low", [P, 3, 2048], F32R)
        ada_raw = sb("ada_raw", [P, 2, 2048])
        y_high = sb("y_high", [P, 8, S], F32R)
        y_low = sb("y_low", [P, 8, S], F32R)
        proj = sb("proj", [P, 32, S])
        tok = sb("tok", [P, TT, 1536])
        temp = sb("temp", [P, 1152])
        probs_t = sb("probs_t", [P, 1152])
        bias_t = sb("bias_t", [P, 2, 768])
        root = sb("root", [P, 512])
        rstd = sb("rstd", [P, 512])
        const = sb("const", [P, CONSTS])
        params = sb("params", [P, PARAMS])
        ada_bias = sb("ada_bias", [P, 4 * 72])
        now = sb("now", [P, NOW])
        c_act = sb("c_act", [P, 5, DT])
        mod_raw = sb("mod_raw", [P, 24])
        mod = sb("mod", [P, 24])
        mod_a = sb("mod_a", [P, DT])
        mod_g = sb("mod_g", [P, DT])
        eps = sb("eps", [P, 1])
        ones = sb("ones", [P, 1])
        zeros = sb("zeros", [P, 512], BF16)
        f_raw = sb("f_raw", [P, DT, 8])
        f_high = sb("f_high", [P, DT, 8], F32R)
        f_low = sb("f_low", [P, DT, 8], F32R)
        f_bias = sb("f_bias", [P, DEPTH, 8])
        f_val = sb("f_val", [P, TT, 8])
        f_abs = sb("f_abs", [P, TT, 8])
        logf = sb("logf", [P, TT, 8])
        cum_q = sb("cum_q", [P, TT, 8])
        cum_k = root[0:8, S:2 * S]
        neg_top = sb("neg_top", [P, 4])
        total = sb("total", [P, 4])
        share = sb("share", [P, 4])

        ident = const[:, ID:ID + P]
        mean_all = const[:, ONES:ONES + P]

        def head_means(t):
            return const[:, BLOCK + 14 - 2 * t:BLOCK + 30 - 2 * t]

        upto = const[:, UPTO:UPTO + S]
        causal = const[:, CAUSAL:CAUSAL + S]

        def head_spread_of(t):
            return bias_t[0:16, t // 4, S + P * (t % 4):S + P * (t % 4) + P]

        flat = lambda a: a.rearrange("p a b -> p (a b)")
        proj_f, temp_f, work_f = flat(proj[:, :, :]), temp[:, :], flat(work[:, :, :])

        pair = [ps(f"pair{i}", [P, 512]) for i in range(2)]
        small = ps("small", [P, 512])
        stat = ps("stat", [P, 512])
        acc = ps("acc", [P, 2048])

        def score_places(b, m):
            if b:
                return acc[:, 1024:1408], acc[:, 0:768]
            bank = 512 * (m % 2)
            return acc[:, bank:bank + P], acc[:, bank + P:bank + 3 * P]

        def logit_places(b, m):
            wide = (P, 3 * P)[b]
            at = 0 if b else 576 * (m % 2)
            return temp[:, at:at + wide], temp[:, at + wide:at + 3 * wide]

        turned = [acc[:, 1536:1920], stat[:, 0:384]]

        third = tuple(16 * n // 3 for n in LAYER_CHUNKS)
        raw_landed = [signal(f"raw_landed{i}", third, 32) for i in range(3)]
        w_high_ready = signal("w_high_ready", LAYER_CHUNKS)
        w_low_ready = signal("w_low_ready", LAYER_CHUNKS, 3)
        chunk_used = signal("chunk_used", LAYER_CHUNKS, 3)
        pair_free = [signal(f"pair_free{i}", tuple(c // 2 for c in COLS), 1) for i in range(2)]
        acc_done = signal("acc_done", (3 * 6, 3 * 5))
        acc_taken = signal("acc_taken", (12, 8))
        ada_landed = [signal(f"ada_landed{i}", (16 * 18,) * 2, 16 * 3) for i in range(2)]
        ada_part = signal("ada_part", (8 * 36, 8 * 36), 8 * len(FIRST_SUMMED))
        ada_used = signal("ada_used", (36, 36), 2 + UNITS)
        ada_copied = signal("ada_copied", (36, 36), 2 + UNITS)
        x_ready = signal("x_ready", (24, 24), 8)
        now_ready = signal("now_ready", (2, 2))
        mod_summed = signal("mod_summed", (3, 3))
        mod_ready = signal("mod_ready", (3, 3))
        squares_ready = signal("squares_ready", (24, 24))
        stat_done = signal("stat_done", (3, 3))
        root_ready = signal("root_ready", (3, 3))
        rstd_ready = signal("rstd_ready", (3, 3))
        scaled_ready = signal("scaled_ready", (24, 24))
        h_high_ready = signal("h_high_ready", (24, 24))
        h_ready = signal("h_ready", (24, 24))
        hidden_high = signal("hidden_high", (22, 22))
        hidden_split = signal("hidden_split", (22, 22))
        scores_done = signal("scores_done", tuple(2 * n for n in HEADS))
        logits_ready = signal("logits_ready", tuple(2 * n for n in HEADS))
        exp_ready = signal("exp_ready", tuple(2 * n for n in HEADS))
        probs_ready = signal("probs_ready", tuple(2 * n for n in HEADS))
        turned_done = signal("turned_done", tuple(t * n for t, n in zip(TURNS, HEADS)))
        turned_ready = signal("turned_ready", tuple(t * n for t, n in zip(TURNS, HEADS)))
        out_done = signal("out_done", HEADS)
        y_high_ready = signal("y_high_ready", HEADS)
        y_ready = signal("y_ready", HEADS)
        bias_landed = [signal(f"bias_landed{i}", (64, 64)) for i in range(2)]
        chain = signal("chain", (2 + 8 * 5 + 8 * 4, 8 * 4 + 4 * 2))
        step_act = signal("step_act", (2, 0))
        side_landed = signal("side_landed", (48, 0))
        pool_d_done = signal("pool_d_done", (1, 0))
        pool_d_ready = signal("pool_d_ready", (4, 0))
        pool_y_done = signal("pool_y_done", (1, 0))
        pool_high = signal("pool_high", (4, 0))
        pool_ready = signal("pool_ready", (4, 0))
        head_sq = signal("head_sq", (8, 0))
        head_stat = signal("head_stat", (8, 0))
        head_root = signal("head_root", (2, 0))
        head_rstd = signal("head_rstd", (2, 0))
        head_spread = signal("head_spread", (2, 0))
        head_normed = signal("head_normed", (8, 0))
        f_split = signal("f_split", (2, 0))
        f_done = signal("f_done", (1, 0))
        f_ready = signal("f_ready", (1, 0))
        cum_done = signal("cum_done", (2, 0))
        cum_ready = signal("cum_ready", (2, 0))
        gates_ready = signal("gates_ready", (2, 1))
        merged_ready = signal("merged_ready", (8, 4))
        out_high_ready = signal("out_high_ready", (4, 4))
        out_split = signal("out_split", (4, 4))
        conv_ready = signal("conv_ready", (0, 4))
        conv_high = signal("conv_high", (0, 4))
        conv_split = signal("conv_split", (0, 4))
        table_stored = signal("table_stored", (80, 0))
        slot_seen = signal("slot_seen", (2, 2))
        const_landed = signal("const_landed", (0, 0))
        rows_landed = signal("rows_landed", (0, 0))
        x_landed = signal("x_landed", (0, 0))
        table_landed = signal("table_landed", (0, 0))
        zeros_ready = signal("zeros_ready", (0, 0))
        params_turned = signal("params_turned", (0, 0))
        params_ready = signal("params_ready", (0, 0))
        table_ready = signal("table_ready", (0, 0))
        tables_stored = signal("tables_stored", (0, 0))
        x_turned = signal("x_turned", (0, 0))
        c_ready = signal("c_ready", (0, 0))
        result_turned = signal("result_turned", (0, 0))
        result_ready = signal("result_ready", (0, 0))
        result_stored = signal("result_stored", (0, 0))

        ada_cols = t["w_ada_all"].rearrange("l (k p) n -> l p k n", p=P)
        gate_cols = t["ffn_gate_all"].rearrange("l i (k p) n -> l i p k n", p=P)
        up_cols = t["ffn_up_all"].rearrange("l i (k p) n -> l i p k n", p=P)
        down_rows = t["ffn_down_all"].rearrange("l i (c k p) n -> l i c p k n", p=P, k=2)
        in_cols = [t["w_in"].rearrange("l (k p) n -> l p k n", p=P),
                   t["w_in_2"].rearrange("l (k p) n -> l p k n", p=P)]
        rows = lambda a: a.rearrange("l (c k p) n -> l c p k n", p=P, k=2)
        branch_rows = t["w_branch"].rearrange("l b (c k p) n -> l b c p k n", p=P, k=2)
        table_store = nc.dram_tensor("table_store", (40, P, TAB), F32, kind="Internal").ap()
        table_rows = bass.AP(tensor=table_store.tensor, offset=P - 1,
                             ap=[[P * TAB, 40], [TAB - 1, P], [1, S]])
        table_groups = [bass.AP(tensor=table_store.tensor, offset=P - 1 + (20 * half + 8) * P * TAB,
                                ap=[[P * TAB, 4], [TAB - 1, P], [4 * P * TAB, 3], [1, S]]) for half in range(2)]
        tables = nc.dram_tensor("tables", (40, TAB), F32, kind="Internal").ap()

        block = ctx.enter_context(nc.Block())

        def cols3(a):
            return a.rearrange("p (k n) -> p k n", k=8)

        def rows3(a):
            return a.rearrange("p (k n) -> p k n", k=2)

        def conv_u():
            return proj_f[:, 0:DT * (S + 2)].rearrange("p (d n) -> p d n", d=DT)

        def wait_taken(eng, at, b, k):
            q = column_no(b, k)
            eng.wait_ge(pair_free[q % 2].sem, pair_free[q % 2].at(at, q // 2 + 1))

        first_slots = ([(ada_raw[:, i, :], ada_landed[i]) for i in range(2)]
                       + [(raw[:, i, :], raw_landed[i]) for i in range(3)])

        @block.sync
        def _(sp):
            def load(at, n, slot, src, extra=None, split=8, settle=False):
                sp.wait_ge(w_low_ready.sem, w_low_ready.at(at, n - 2, extra))
                if settle:
                    sp.sem_inc(slot_seen.sem, 1)
                dst = raw[:, slot, :]
                sp.dma_start(cols3(dst) if split == 8 else rows3(dst), src).then_inc(raw_landed[slot].sem, 16)

            def load_ada(at, u, slot, src, extra=None):
                sp.wait_ge(ada_used.sem, ada_used.at(at, u - 1, extra))
                sp.dma_start(cols3(ada_raw[:, slot, :]), src).then_inc(ada_landed[slot].sem, 16)

            sp.dma_start(flat(proj[:, 16:24, :])[0:120, 0:P], t["rows_a"]).then_inc(rows_landed.sem, 16)
            sp.dma_start(flat(proj[:, 16:24, :])[0:64, P:2 * P], t["rows_b"]).then_inc(rows_landed.sem, 16)
            sp.dma_start(const[:, :], t["const"]).then_inc(const_landed.sem, 16)
            for i in range(2):
                sp.dma_start(bias_t[0:16, i, S:3 * S], t["head_rows"][:, 512 * i:512 * i + 512]
                             ).then_inc(const_landed.sem, 16)
            for u in range(UNITS):
                if u >= FIRST_RING:
                    sp.wait_ge(ada_used.sem, 2 + u - FIRST_RING + 1)
                sp.dma_start(cols3(first_slots[u % FIRST_RING][0]), ada_cols[0, :, :, u * 256:u * 256 + 256]
                             ).then_inc(first_slots[u % FIRST_RING][1].sem, 16)
            sp.wait_ge(tables_stored.sem, 64)
            sp.wait_ge(ada_used.sem, 2 + 10)
            load((0, 0), 0, 0, gate_cols[0, 0, :, :, 0:256])
            load((0, 0), 1, 1, up_cols[0, 0, :, :, 0:256])
            for b in range(2):
                with sp.Fori(0, DEPTH) as l:
                    at = (b, l)

                    def ada_src(stage, u, extra=None):
                        g = (stage + 1) % 3
                        first = g * 3 * D + u * 256
                        if stage < 2:
                            layer = l + 2 * b
                        else:
                            layer = 3 if b else l + 1
                        start = first if extra is None else extra + first
                        return ada_cols[layer, :, :, bass.ds(start, 256)]

                    def ffn_loads(i):
                        stage, c = 2 * i, i * (MIX + MIX_CHUNKS[b])
                        if i == 1:
                            load(at, c, 0, gate_cols[l + 2 * b, i, :, :, 0:256])
                            load(at, c + 1, 1, up_cols[l + 2 * b, i, :, :, 0:256])
                        load_ada(at, 12 * stage, 0, ada_src(stage, 0))
                        with sp.Fori(0, (TRIPS - 1) // 2) as r:
                            for half in range(2):
                                first = r * 512 + 256 * (1 + half)
                                load(at, c + 2 + 3 * half, 2, gate_cols[l + 2 * b, i, :, :, bass.ds(first, 256)], r * 6)
                                load(at, c + 3 + 3 * half, 0, up_cols[l + 2 * b, i, :, :, bass.ds(first, 256)], r * 6)
                                load(at, c + 4 + 3 * half, 1, down_rows[l + 2 * b, i, r * 2 + half], r * 6, split=2)
                                load_ada(at, 12 * stage + 1 + half, (1 + half) % 2,
                                         ada_src(stage, 1 + half, r * 512), r * 2)
                            if b == 0 and i == 0:
                                first_table = l * 20 + r * 4
                                sp.dma_start(table_store[bass.ds(first_table, 4)],
                                             tables[bass.ds(first_table, 4)].unsqueeze(1).to_broadcast([4, P, TAB])
                                             ).then_inc(table_stored.sem, 16)
                        load_ada(at, 12 * stage + UNITS - 1, 1, ada_src(stage, UNITS - 1))
                        load(at, c + FFN_CHUNKS - 1, 2, down_rows[l + 2 * b, i, TRIPS - 1], split=2)
                        if i == 1:
                            follow = 3 if b else l + 1
                            load(at, LAYER_CHUNKS[b], 0, gate_cols[follow, 0, :, :, 0:256])
                            load(at, LAYER_CHUNKS[b] + 1, 1, up_cols[follow, 0, :, :, 0:256])

                    ffn_loads(0)
                    for k, (kind, a) in enumerate(MIXES[b]):
                        if kind in ROW_KINDS:
                            src = {"wb": lambda: branch_rows[l, 1, a], "wa": lambda: branch_rows[l, 0, a],
                                   "wc": lambda: branch_rows[l, 2, a],
                                   "wo": lambda: rows(t["w_o_2"] if b else t["w_out"])[l, a],
                                   "wconv": lambda: rows(t["w_conv_out_2"])[l, a],
                                   "wattn": lambda: rows(t["w_attn_out_2"])[l, a]}[kind]()
                            load(at, MIX + k, k % 3, src, split=2, settle=a == 0)
                        else:
                            load(at, MIX + k, k % 3, in_cols[b][l, :, :, a:a + 256], settle=a == 0)
                        u = unit_behind(b, k)
                        if u is not None:
                            load_ada(at, 12 + u, u % 2, ada_src(1, u))
                    ffn_loads(1)
            sp.wait_ge(result_ready.sem, 4)
            sp.dma_start(out.rearrange("b (t p) n -> p (b t) n", p=P),
                         proj_f[:, 0:2 * D].rearrange("p (t n) -> p t n", t=TT)).then_inc(result_stored.sem, 16)
            sp.wait_ge(result_stored.sem, 16)

        @block.scalar
        def _(act):
            def high(at, n, slot, extra=None):
                turn = raw_landed[slot].at(at, 16 * (n // 3 + 1), None if extra is None else extra * 32)
                act.wait_ge(raw_landed[slot].sem, turn)
                act.wait_ge(chunk_used.sem, chunk_used.at(at, n - 2, None if extra is None else extra * 6))
                nc.scalar.activation(w_high[:, slot, :], raw[:, slot, :], ACT.Copy).then_inc(w_high_ready.sem, 1)

            def copy_ada(at, u, parity, dst, extra=None):
                act.wait_ge(ada_used.sem, ada_used.at(at, u + 1, extra) if at != "start" else u + 3)
                nc.scalar.activation(dst, small[:, 2 * parity:2 * parity + 2], ACT.Copy).then_inc(ada_copied.sem, 1)

            def squares(at, s):
                for d in range(DT):
                    act.wait_ge(x_ready.sem, x_ready.at(at, DT * (s - 1) + d + 1))
                    nc.scalar.activation(work[:, d, :], x[:, d, :], ACT.Square).then_inc(squares_ready.sem, 1)

            def norm(at, s, third):
                squares(at, s)
                act.wait_ge(stat_done.sem, stat_done.at(at, s + 1))
                nc.scalar.activation(root[:, 0:S], stat[:, 0:S], ACT.Sqrt, bias=eps[:, 0:1]).then_inc(root_ready.sem, 1)
                high(at, third, 2)
                for d in range(DT):
                    act.wait_ge(scaled_ready.sem, scaled_ready.at(at, DT * s + d + 1))
                    nc.scalar.activation(h_high[:, d, :], work[:, d, :], ACT.Identity,
                                         bias=mod[:, d:d + 1]).then_inc(h_high_ready.sem, 1)

            act.dma_start(work_f.rearrange("p (t n) -> p t n", t=TT),
                          t["x"].rearrange("b (t p) n -> p (b t) n", p=P)).then_inc(x_landed.sem, 16)
            for i in range(3):
                act.dma_start(flat(proj[:, 16:24, :])[0:96, (2 + i) * P:(3 + i) * P],
                              t["rows_ada"][96 * i:96 * i + 96, :]).then_inc(rows_landed.sem, 16)
            act.dma_start(proj_f[0:16, P - 1:P - 1 + REL], t["rel_rows"]).then_inc(table_landed.sem, 16)
            act.dma_start(proj_f[0:32, TAB:TAB + 24], t["rel_bias_2"]).then_inc(table_landed.sem, 16)
            act.dma_start(proj_f[0:32, 2 * TAB:3 * TAB], t["one_hot"]).then_inc(table_landed.sem, 16)
            act.dma_start(proj_f[0:24, 3 * TAB:4 * TAB], t["distance_mask"]).then_inc(table_landed.sem, 16)
            act.dma_start(flat(f_bias[:, :, :]), t["forget_bias"].rearrange("l h -> (l h)").partition_broadcast(P)
                          ).then_inc(table_landed.sem, 16)
            act.wait_ge(params_ready.sem, 2)
            for i, src in ((0, CVEC), (1, CVEC), (2, CVEC + DT), (3, CVEC + DT), (4, CVEC + DT)):
                nc.scalar.activation(c_act[:, i, :], params[:, src:src + DT], ACT.Silu).then_inc(c_ready.sem, 1)
            for i in range(4):
                g = params[:, QKG + 2 * i:QKG + 2 * i + 1]
                nc.scalar.activation(g, g, ACT.Copy, scale=HEAD ** -0.5).then_inc(c_ready.sem, 1)
            for u in range(UNITS):
                copy_ada("start", u, u % 2, mod_raw[:, 2 * u:2 * u + 2])
                if u == 3:
                    act.wait_ge(table_ready.sem, 2)
                    for layer in range(2):
                        act.dma_start(tables[20 * layer:20 * layer + 8], proj_f[8 * layer:8 * layer + 8, 0:TAB]
                                      ).then_inc(tables_stored.sem, 16)
                        act.dma_start(tables[20 * layer + 8:20 * layer + 20],
                                      proj_f[12 * layer:12 * layer + 12, 4 * TAB:5 * TAB]).then_inc(tables_stored.sem, 16)
            act.wait_ge(tables_stored.sem, 64)
            high((0, 0), 0, 0)
            high((0, 0), 1, 1)

            for b in range(2):
                with act.Fori(0, DEPTH) as l:
                    at = (b, l)

                    def ffn_act(i):
                        stage, c = 2 * i, i * (MIX + MIX_CHUNKS[b])
                        y0, q0 = TRIPS * i, i * (COLS[b] - 2 * TRIPS)

                        def silu(j, extra=None):
                            act.wait_ge(chunk_used.sem, chunk_used.at(
                                at, c + 1 + (3 * j - 1 if j else 0), None if extra is None else extra * 6))
                            nc.scalar.activation(temp[:, 0:512], pair[0][:, :], ACT.Silu).then_inc(pair_free[0].sem, 1)

                        def hidden(j, parity, extra=None):
                            act.wait_ge(pair_free[1].sem, pair_free[1].at(
                                at, q0 // 2 + j + 1, None if extra is None else extra * 2))
                            nc.scalar.activation(flat(y_high[:, 2 * parity:2 * parity + 2, :]), temp[:, 512:1024],
                                                 ACT.Copy).then_inc(hidden_high.sem, 1)

                        norm(at, stage, c + 2)
                        silu(0)
                        hidden(0, 0)
                        with act.Fori(0, (TRIPS - 1) // 2) as r:
                            for half in range(2):
                                j = 1 + half
                                high(at, c + 3 * j, 0, r)
                                high(at, c + 3 * j + 1, 1, r)
                                copy_ada(at, 12 * stage + j - 1, (j - 1) % 2,
                                         mod_raw[:, bass.ds(r * 4 + 2 * (j - 1), 2)], r * 2)
                                silu(j, r)
                                high(at, c + 3 * j + 2, 2, r)
                                hidden(j, j % 2, r)
                        high(at, MIX if i == 0 else LAYER_CHUNKS[b], 0)
                        high(at, (MIX if i == 0 else LAYER_CHUNKS[b]) + 1, 1)
                        copy_ada(at, 12 * stage + UNITS - 2, 0, mod_raw[:, 2 * UNITS - 4:2 * UNITS - 2])
                        copy_ada(at, 12 * stage + UNITS - 1, 1, mod_raw[:, 2 * UNITS - 2:2 * UNITS])

                    def product_ready(k):
                        act.wait_ge(chunk_used.sem, chunk_used.at(at, MIX + k + 1))

                    def attention_act(copy_gate):
                        wide, turns = (P, 3 * P)[b], TURNS[b]
                        biased = 8

                        def out_part(m):
                            act.wait_ge(out_done.sem, out_done.at(at, m + 1))
                            tile, r0 = m // 2, HEAD * (m % 2)
                            nc.scalar.activation(y_high[r0:r0 + HEAD, tile, :], small[r0:r0 + HEAD, S:2 * S],
                                                 ACT.Copy).then_inc(y_high_ready.sem, 1)

                        act.wait_ge(table_stored.sem, 160 if b else table_stored.at(at, 80))
                        for i in range(2):
                            bias_load(i)
                        for i in range(HEADS[b] + VALUE_STEP[b]):
                            if b and i >= VALUE_STEP[b]:
                                out_part(i - VALUE_STEP[b])
                            m = i - TURN_STEP[b]
                            if 0 <= m < HEADS[b]:
                                o = 0 if b else 576 * (m % 2)
                                for part in range(turns):
                                    n = turns * m + part
                                    w = 3 * wide // turns
                                    act.wait_ge(turned_done.sem, turned_done.at(at, n + 1))
                                    nc.scalar.activation(probs_t[:, o + w * part:o + w * part + w],
                                                         turned[n % 2][:, 0:w], ACT.Copy
                                                         ).then_inc(turned_ready.sem, 1)
                            if i < HEADS[b]:
                                for half, L in enumerate(logit_places(b, i)):
                                    s = 2 * (i % 2) + half
                                    act.wait_ge(logits_ready.sem, logits_ready.at(at, 2 * i + half + 1))
                                    nc.scalar.activation(L, L, ACT.Exp, bias=neg_top[:, s:s + 1],
                                                         accum_out=total[:, s:s + 1]).then_inc(exp_ready.sem, 1)
                                if i + 2 < biased:
                                    bias_load(i + 2)
                            if not b and i >= VALUE_STEP[b]:
                                out_part(i - VALUE_STEP[b])
                            if i % 2 == 0 and i <= HEADS[b]:
                                k = GATES_FROM[b] + i // 2
                                if i > 0:
                                    copy_gate(k - 1)
                                if i < HEADS[b]:
                                    high(at, MIX + k + 2, (k + 2) % 3)

                    def bias_load(i):
                        src = table_groups[i // 4][i % 4] if b else table_rows[l * 20 + i]
                        dst = bias_t[:, i % 2, :]
                        dst = dst.rearrange("p (g n) -> p g n", g=3) if b else dst[:, 0:S]
                        act.dma_start(dst, src).then_inc(bias_landed[i % 2].sem, 16)

                    def unit(k):
                        u = unit_behind(b, k)
                        if u is not None:
                            copy_ada(at, 12 + u, u % 2, mod_raw[:, 2 * u:2 * u + 2])

                    def evacuate(k, q, dst, func=ACT.Copy, scale=1.0, done=None, src=None):
                        product_ready(k)
                        nc.scalar.activation(dst, pair[q % 2][:, :] if src is None else src, func, scale=scale
                                             ).then_inc((done or pair_free[q % 2]).sem, 1)

                    def out_high(bank):
                        act.wait_ge(merged_ready.sem, merged_ready.at(at, (4 if b == 0 else 0) + bank + 1))
                        nc.scalar.activation(flat(h_high[:, 2 * bank:2 * bank + 2, :]),
                                             work_f[:, 512 * bank:512 * bank + 512], ACT.Copy
                                             ).then_inc(out_high_ready.sem, 1)

                    ffn_act(0)
                    norm(at, 1, MIX + 2)
                    q = 2 * TRIPS
                    if b == 0:
                        act.dma_start(proj_f[:, 0:1536], t["pool_mats"]).then_inc(side_landed.sem, 16)
                        act.dma_start(proj_f[:, 1536:2048].rearrange("p (g e) -> p g e", g=4),
                                      t["w_pool"].rearrange("l g c e -> l c g e")[l]).then_inc(side_landed.sem, 16)
                        act.dma_start(f_raw[:, :, :], in_cols[0][l, :, :, F_LIN:F_LIN + 8]).then_inc(side_landed.sem, 16)
                        for k, (kind, a) in enumerate(MIX1):
                            if kind == "g":
                                break
                            if k > 0:
                                high(at, MIX + k + 2, (k + 2) % 3)
                            if kind == "u":
                                product_ready(k)
                                nc.scalar.activation(tok[:, :, 512 + 256 * k:768 + 256 * k],
                                                     pair[q % 2][:, :].rearrange("p (t n) -> p t n", t=2),
                                                     ACT.Copy).then_inc(pair_free[q % 2].sem, 1)
                            if kind == "gb":
                                evacuate(k, q, flat(proj[:, 16 + 2 * (k - 2):18 + 2 * (k - 2), :]),
                                         ACT.Sigmoid)
                            if kind in "qk":
                                if head_no(k) >= 1:
                                    act.wait_ge(head_stat.sem, head_stat.at(at, head_no(k)))
                                evacuate(k, q, temp[:, 0:512], ACT.Square, done=head_sq)
                            if k in (12, 18):
                                group = (k - 12) // 6
                                act.wait_ge(head_stat.sem, head_stat.at(at, 4 * group + 4))
                                w = slice(S * group, S * group + S)
                                nc.scalar.activation(root[0:16, w], stat[0:16, w], ACT.Sqrt, bias=eps[0:16, 0:1]
                                                     ).then_inc(head_root.sem, 1)
                            if k == 4:
                                for g in range(4):
                                    act.wait_ge(pool_y_done.sem, pool_y_done.at(at, 1))
                                    nc.scalar.activation(y_high[:, g, :], acc[:, 512 * g + S:512 * g + 2 * S],
                                                         ACT.Copy, scale=now[:, NOW_POOL + g:NOW_POOL + g + 1]
                                                         ).then_inc(pool_high.sem, 1)
                            if k == 9:
                                act.wait_ge(side_landed.sem, side_landed.at(at, 48))
                                nc.scalar.activation(flat(f_high[:, :, :]), flat(f_raw[:, :, :]), ACT.Copy
                                                     ).then_inc(f_split.sem, 1)
                            unit(k)
                            q += kind not in ROW_KINDS
                        act.wait_ge(chain.sem, chain.at(at, 2))
                        nc.scalar.activation(flat(f_abs[:, :, :]), flat(f_abs[:, :, :]), ACT.Exp, scale=-1.0
                                             ).then_inc(step_act.sem, 1)
                        act.wait_ge(step_act.sem, step_act.at(at, 1))
                        nc.scalar.activation(flat(f_abs[:, :, :]), flat(f_abs[:, :, :]), ACT.Ln, bias=1.0
                                             ).then_inc(step_act.sem, 1)

                        def copy_gate1(k):
                            i = k - 20
                            evacuate(k, column_no(b, k), flat(proj[:, 16 + 2 * i:18 + 2 * i, :]))
                        attention_act(copy_gate1)
                        rest = range(28, 36)
                    else:
                        for k, (kind, a) in enumerate(MIX2):
                            if kind == "g":
                                break
                            if k > 0:
                                high(at, MIX + k + 2, (k + 2) % 3)
                            if kind == "cc":
                                if k >= 2:
                                    wait_taken(act, at, b, k - 1)
                                evacuate(k, q, temp[:, 0:512])
                            if kind == "cb":
                                i = k - 8
                                wait_taken(act, at, b, k)
                                nc.scalar.activation(flat(y_high[:, 2 * i:2 * i + 2, :]), temp[:, 512:1024], ACT.Copy
                                                     ).then_inc(conv_high.sem, 1)
                            if kind == "gc":
                                i = k - 12
                                evacuate(k, q, flat(proj[:, 24 + 2 * i:26 + 2 * i, :]), ACT.Sigmoid)
                            if kind == "q":
                                i = k - 20
                                evacuate(k, q, flat(proj[:, 2 * i:2 * i + 2, :]), scale=HEAD ** -0.5)
                            if kind == "k":
                                i = k - 26
                                evacuate(k, q, flat(proj[:, 12 + 2 * i:14 + 2 * i, :]))
                            if kind == "v":
                                i = k - 32
                                evacuate(k, q, tok[:, :, 256 * i:256 * i + 256],
                                         src=pair[q % 2][:, :].rearrange("p (t n) -> p t n", t=2))
                            unit(k)
                            q += kind not in ROW_KINDS

                        def copy_gate2(k):
                            i = k - 38
                            evacuate(k, column_no(b, k), flat(proj[:, 24 + 2 * i:26 + 2 * i, :]))
                        attention_act(copy_gate2)
                        rest = range(42, 48)
                    for k in rest:
                        high(at, MIX + k + 2, (k + 2) % 3)
                        if k - rest[0] < (2, 1)[b]:
                            first = (16, 24)[b] + 8 * (k - rest[0])
                            g = flat(proj[:, first:first + 8, :])
                            wait_taken(act, at, b, rest[0] - 2)
                            wait_taken(act, at, b, rest[0] - 1)
                            nc.scalar.activation(g, g, ACT.Sigmoid).then_inc(gates_ready.sem, 1)
                        if k == MIX_CHUNKS[b] - 5:
                            for bank in range(4):
                                out_high(bank)
                        unit(k)
                    ffn_act(1)

            squares("end", 0)
            act.wait_ge(stat_done.sem, stat_done.at("end", 1))
            nc.scalar.activation(root[:, 0:S], stat[:, 0:S], ACT.Sqrt, bias=eps[:, 0:1]).then_inc(root_ready.sem, 1)

        @block.gpsimd
        def _(pool):
            pool.memset(eps[:, :], EPS).then_inc(zeros_ready.sem, 1)
            pool.memset(zeros[:, :], 0.0).then_inc(zeros_ready.sem, 1)
            pool.wait_ge(c_ready.sem, 9)
            for b in range(2):
                with pool.Fori(0, DEPTH) as l:
                    at = (b, l)
                    copies = [(NOW_GAIN, 24, params[:, bass.ds(l * 24 + (GAIN + 48 * b), 24)]),
                              (NOW_BIAS, 72, ada_bias[:, bass.ds(l * 72 + 144 * b, 72)])]
                    if b == 0:
                        copies += [(NOW_QK, 4, params[:, bass.ds(l * 4 + QKG, 4)]),
                                   (NOW_POOL, 4, params[:, bass.ds(l * 4 + POOLS, 4)])]
                    else:
                        copies += [(NOW_CONV, 24, params[:, bass.ds(l * 24 + CONVW, 24)])]
                    pool.wait_ge(x_ready.sem, x_ready.at(at, 0))
                    for first, n, src in copies:
                        pool.tensor_copy(now[:, first:first + n], src)
                    pool.tensor_copy(now[:, NOW_C:NOW_C + DT], c_act[:, l + 2 * b, :]).then_inc(now_ready.sem, 1)
                    pool.wait_ge(x_ready.sem, x_ready.at(at, 16))
                    pool.tensor_copy(now[:, NOW_C:NOW_C + DT], c_act[:, l + 2 * b + 1, :]
                                     ).then_inc(now_ready.sem, 1)

        @block.vector
        def _(dve):
            def low(at, n, slot, extra=None):
                dve.wait_ge(w_high_ready.sem, w_high_ready.at(at, n + 1, None if extra is None else extra * 6))
                nc.vector.tensor_tensor(w_low[:, slot, :], raw[:, slot, :], w_high[:, slot, :].bitcast(F32),
                                        ALU.subtract).then_inc(w_low_ready.sem, 1)

            links = [0]

            def linked(ins, at):
                links[0] += 1
                ins.then_inc(chain.sem, 1)
                dve.wait_ge(chain.sem, chain.at(at, links[0]))

            def row_tiles_sum(w, cvec, part):
                nc.vector.tensor_scalar(w[:, 0, :], w[:, 0, :], cvec[:, 0:1], None, ALU.mult
                                        ).then_inc(ada_part.sem, 1)
                for k in range(1, DT):
                    dve.wait_ge(ada_part.sem, part(k))
                    nc.vector.scalar_tensor_tensor(out=w[:, 0, :], in0=w[:, k, :], scalar=cvec[:, k:k + 1],
                                                   in1=w[:, 0, :], op0=ALU.mult, op1=ALU.add
                                                   ).then_inc(ada_part.sem, 1)

            def ada_sum(at, u, slot, trips=None):
                step = None if trips is None else trips * 16
                dve.wait_ge(ada_landed[slot].sem, ada_landed[slot].at(at, 16 * (u // 2 + 1), step))
                row_tiles_sum(cols3(ada_raw[:, slot, :]), now[:, NOW_C:NOW_C + DT],
                              lambda k: ada_part.at(at, DT * u + k, step))

            def modulation(at, s):
                dve.wait_ge(ada_copied.sem, ada_copied.at(at, 12 * s))
                if s == 0:
                    dve.wait_ge(now_ready.sem, now_ready.at(at, 1))
                dve.wait_ge(x_ready.sem, x_ready.at(at, 8 * s))
                nc.vector.tensor_tensor(mod[:, :], mod_raw[:, :], now[:, NOW_BIAS + 24 * s:NOW_BIAS + 24 * s + 24],
                                        ALU.add).then_inc(mod_summed.sem, 1)
                dve.wait_ge(mod_summed.sem, mod_summed.at(at, s + 1))
                nc.vector.scalar_tensor_tensor(out=mod_a[:, :], in0=mod[:, 8:16], scalar=1.0,
                                               in1=now[:, NOW_GAIN + 8 * s:NOW_GAIN + 8 * s + 8],
                                               op0=ALU.add, op1=ALU.mult)
                nc.vector.tensor_scalar(mod_g[:, :], mod[:, 16:24], 1.0 if s == 1 else 0.5, None,
                                        ALU.mult).then_inc(mod_ready.sem, 1)

            def norm(at, s, second):
                modulation(at, s)
                low(at, second, 1)
                dve.wait_ge(root_ready.sem, root_ready.at(at, s + 1))
                nc.vector.reciprocal(rstd[:, 0:S], root[:, 0:S]).then_inc(rstd_ready.sem, 1)
                dve.wait_ge(rstd_ready.sem, rstd_ready.at(at, s + 1))
                dve.wait_ge(mod_ready.sem, mod_ready.at(at, s + 1))

                def rest(d):
                    dve.wait_ge(h_high_ready.sem, h_high_ready.at(at, DT * s + d + 1))
                    nc.vector.scalar_tensor_tensor(out=h_low[:, d, :], in0=work[:, d, :], scalar=mod[:, d:d + 1],
                                                   in1=h_high[:, d, :].bitcast(F32), op0=ALU.add,
                                                   op1=ALU.subtract).then_inc(h_ready.sem, 1)
                for d in range(DT):
                    nc.vector.scalar_tensor_tensor(out=work[:, d, :], in0=x[:, d, :], scalar=mod_a[:, d:d + 1],
                                                   in1=rstd[:, 0:S], op0=ALU.mult, op1=ALU.mult
                                                   ).then_inc(scaled_ready.sem, 1)
                    if d >= 1:
                        rest(d - 1)
                rest(DT - 1)

            def update(at, n_last, a0):
                for d in range(DT):
                    acc_wait(at, n_last, a0, d // 2)
                    nc.vector.scalar_tensor_tensor(out=x[:, d, :], in0=acc[:, S * d:S * d + S],
                                                   scalar=mod_g[:, d:d + 1], in1=x[:, d, :],
                                                   op0=ALU.mult, op1=ALU.add).then_inc(x_ready.sem, 1)

            def acc_wait(at, n_last, a0, bank):
                if bank < 3:
                    dve.wait_ge(acc_done.sem, acc_done.at(at, 3 * a0 + bank + 1))
                else:
                    dve.wait_ge(chunk_used.sem, chunk_used.at(at, n_last + 1))

            nc.vector.memset(ones[:, :], 1.0).then_inc(zeros_ready.sem, 1)
            dve.wait_ge(params_turned.sem, 1)
            nc.vector.tensor_copy(params[:, :], pair[0][:, 0:PARAMS]).then_inc(params_ready.sem, 1)
            nc.vector.tensor_copy(ada_bias[:, :], pair[1][:, 0:4 * 72]).then_inc(params_ready.sem, 1)
            dve.wait_ge(c_ready.sem, 1)
            for n, u in enumerate(FIRST_SUMMED):
                slot, landed = first_slots[u % FIRST_RING]
                dve.wait_ge(landed.sem, 16 * (u // FIRST_RING + 1))
                row_tiles_sum(cols3(slot), c_act[:, 0, :], lambda k: DT * n + k)
                if n == 3:
                    dve.wait_ge(table_landed.sem, 80)
                    nc.vector.tensor_copy(proj_f[0:16, 0:P - 1], proj_f[0:16, P - 1:P].to_broadcast([16, P - 1])
                                          ).then_inc(table_ready.sem, 1)
                    dve.wait_ge(params_turned.sem, 2)
                    nc.vector.tensor_tensor(proj_f[0:24, 4 * TAB:5 * TAB], stat[0:24, 0:TAB],
                                            proj_f[0:24, 3 * TAB:4 * TAB], ALU.add).then_inc(table_ready.sem, 1)
                    for d in range(DT):
                        dve.wait_ge(x_turned.sem, 1)
                        nc.vector.tensor_copy(x[:, d, :], acc[:, S * d:S * d + S]).then_inc(x_ready.sem, 1)
            low((0, 0), 0, 0)

            for b in range(2):
                with dve.Fori(0, DEPTH) as l:
                    at = (b, l)
                    links[0] = 0

                    def ffn_dve(i):
                        stage, c = 2 * i, i * (MIX + MIX_CHUNKS[b])
                        y0, q0 = TRIPS * i, i * (COLS[b] - 2 * TRIPS)

                        def hidden(j, parity, extra=None):
                            e2 = None if extra is None else extra * 2
                            dve.wait_ge(pair_free[0].sem, pair_free[0].at(at, q0 // 2 + j + 1, e2))
                            dve.wait_ge(chunk_used.sem, chunk_used.at(
                                at, c + 1 + (3 * j if j else 1), None if extra is None else extra * 6))
                            nc.vector.tensor_tensor(temp[:, 512:1024], temp[:, 0:512], pair[1][:, :], ALU.mult
                                                    ).then_inc(pair_free[1].sem, 1)
                            dve.wait_ge(hidden_high.sem, hidden_high.at(at, y0 + j + 1, e2))
                            nc.vector.tensor_tensor(flat(y_low[:, 2 * parity:2 * parity + 2, :]), temp[:, 512:1024],
                                                    flat(y_high[:, 2 * parity:2 * parity + 2, :]).bitcast(F32),
                                                    ALU.subtract).then_inc(hidden_split.sem, 1)

                        norm(at, stage, c + 1)
                        dve.wait_ge(now_ready.sem, now_ready.at(at, 1 + i))
                        ada_sum(at, 12 * stage, 0)
                        low(at, c + 2, 2)
                        hidden(0, 0)
                        with dve.Fori(0, (TRIPS - 1) // 2) as r:
                            for half in range(2):
                                j = 1 + half
                                low(at, c + 3 * j, 0, r)
                                low(at, c + 3 * j + 1, 1, r)
                                ada_sum(at, 12 * stage + j, j % 2, r)
                                low(at, c + 3 * j + 2, 2, r)
                                hidden(j, j % 2, r)
                        ada_sum(at, 12 * stage + UNITS - 1, 1)
                        low(at, MIX if i == 0 else LAYER_CHUNKS[b], 0)
                        update(at, c + FFN_CHUNKS - 1, 0 if i == 0 else (5 if b == 0 else 4))

                    def product_ready(k):
                        dve.wait_ge(chunk_used.sem, chunk_used.at(at, MIX + k + 1))

                    def attention_dve():
                        G = GROUPS2 if b else 1
                        v = "p (g n) -> p g n"

                        def out_part(m):
                            tile, r0 = m // 2, HEAD * (m % 2)
                            dve.wait_ge(y_high_ready.sem, y_high_ready.at(at, m + 1))
                            nc.vector.tensor_tensor(y_low[r0:r0 + HEAD, tile, :], small[r0:r0 + HEAD, S:2 * S],
                                                    y_high[r0:r0 + HEAD, tile, :].bitcast(F32), ALU.subtract
                                                    ).then_inc(y_ready.sem, 1)

                        def logits(m):
                            forget = m >= 8
                            ago = TURN_STEP[b]
                            if m >= ago:
                                dve.wait_ge(turned_done.sem, turned_done.at(at, TURNS[b] * (m - ago + 1)))
                            if not forget:
                                dve.wait_ge(bias_landed[m % 2].sem, bias_landed[m % 2].at(at, 16 * (m // 2 + 1)))
                            if b == 0 and not forget:
                                linked(nc.vector.memset(bias_t[0:HEAD, m % 2, 192:256], NEG), at)
                            for half, (sc, L) in enumerate(zip(score_places(b, m), logit_places(b, m))):
                                s = 2 * (m % 2) + half
                                dve.wait_ge(scores_done.sem, scores_done.at(at, 2 * m + (half + 1 if b else 2)))
                                if forget:
                                    bias = causal[:, 128:256] if half == 0 else causal[:, 0:256]
                                    linked(nc.vector.scalar_tensor_tensor(
                                        out=L, in0=sc, scalar=cum_q[:, half, m - 8:m - 7], in1=bias,
                                        op0=ALU.add, op1=ALU.add), at)
                                else:
                                    bias = bias_t[:, m % 2, 0:G * S].rearrange(v, g=G)
                                    if half == 0:
                                        bias = bias[:, :, 128:256]
                                    linked(nc.vector.tensor_tensor(L.rearrange(v, g=G), sc.rearrange(v, g=G),
                                                                   bias, ALU.add), at)
                                nc.vector.tensor_reduce(neg_top[:, s:s + 1], L, AX_X, ALU.max,
                                                        negate=True).then_inc(logits_ready.sem, 1)

                        def normalize(m):
                            for half, L in enumerate(logit_places(b, m)):
                                s = 2 * (m % 2) + half
                                dve.wait_ge(exp_ready.sem, exp_ready.at(at, 2 * m + half + 1))
                                linked(nc.vector.reciprocal(share[:, s:s + 1], total[:, s:s + 1]), at)
                                nc.vector.tensor_scalar(L, L, share[:, s:s + 1], None, ALU.mult
                                                        ).then_inc(probs_ready.sem, 1)

                        for i in range(HEADS[b] + VALUE_STEP[b]):
                            if b and i >= VALUE_STEP[b]:
                                out_part(i - VALUE_STEP[b])
                            if i < HEADS[b]:
                                logits(i)
                            if not b and 1 <= i <= HEADS[b]:
                                normalize(i - 1)
                            if not b and i == 4:
                                dve.wait_ge(cum_done.sem, cum_done.at(at, 2))
                                nc.vector.tensor_copy(flat(cum_q[:, :, :]), small[:, 32:48]
                                                      ).then_inc(cum_ready.sem, 1)
                                nc.vector.tensor_scalar(cum_k, small[0:8, S:2 * S], -1.0, None, ALU.mult
                                                        ).then_inc(cum_ready.sem, 1)
                                dve.wait_ge(cum_ready.sem, cum_ready.at(at, 2))
                            if not b and i >= VALUE_STEP[b]:
                                out_part(i - VALUE_STEP[b])
                            if i % 2 and i < HEADS[b]:
                                k = GATES_FROM[b] + i // 2
                                low(at, MIX + k + 2, (k + 2) % 3)
                            if b and i < HEADS[b]:
                                normalize(i)

                    def merge(k, a0, taken, gate_tile, first=False, gates=0, last=False):
                        if first:
                            wait_taken(dve, at, b, (4, 14)[b])
                            wait_taken(dve, at, b, (5, 15)[b])
                        else:
                            dve.wait_ge(gates_ready.sem, gates_ready.at(at, gates))
                        for bank in range(4):
                            acc_wait(at, MIX + k, a0, bank)
                            w = slice(512 * bank, 512 * bank + 512)
                            g = flat(proj[:, gate_tile + 2 * bank:gate_tile + 2 * bank + 2, :])
                            if first:
                                nc.vector.tensor_tensor(work_f[:, w], acc[:, w], g, ALU.mult
                                                        ).then_inc(acc_taken.sem, 1)
                            else:
                                nc.vector.tensor_tensor(temp[:, 0:512] if bank % 2 else temp[:, 512:1024],
                                                        acc[:, w], g, ALU.mult).then_inc(acc_taken.sem, 1)
                                dve.wait_ge(acc_taken.sem, acc_taken.at(at, taken + bank + 1))
                                nc.vector.tensor_tensor(work_f[:, w], work_f[:, w],
                                                        temp[:, 0:512] if bank % 2 else temp[:, 512:1024],
                                                        ALU.add).then_inc(merged_ready.sem, 1)
                            if last and bank >= 1:
                                out_low(bank - 1)
                        if last:
                            out_low(3)

                    def out_low(bank):
                        dve.wait_ge(out_high_ready.sem, out_high_ready.at(at, bank + 1))
                        nc.vector.tensor_tensor(flat(h_low[:, 2 * bank:2 * bank + 2, :]),
                                                work_f[:, 512 * bank:512 * bank + 512],
                                                flat(h_high[:, 2 * bank:2 * bank + 2, :]).bitcast(F32),
                                                ALU.subtract).then_inc(out_split.sem, 1)

                    def unit(k):
                        u = unit_behind(b, k + 2)
                        if u is not None:
                            ada_sum(at, 12 + u, u % 2)

                    ffn_dve(0)
                    norm(at, 1, MIX + 1)
                    q = 2 * TRIPS
                    if b == 0:
                        for k, (kind, a) in enumerate(MIX1):
                            if kind == "g":
                                break
                            low(at, MIX + k + 2, (k + 2) % 3)
                            unit(k)
                            if k == 3:
                                for g in range(4):
                                    dve.wait_ge(pool_d_done.sem, pool_d_done.at(at, 1))
                                    nc.vector.tensor_copy(proj[:, 8 + g, :], acc[:, 512 * g:512 * g + S]
                                                          ).then_inc(pool_d_ready.sem, 1)
                            if k == 4:
                                for g in range(4):
                                    dve.wait_ge(pool_high.sem, pool_high.at(at, g + 1))
                                    nc.vector.scalar_tensor_tensor(
                                        out=y_low[:, g, :], in0=acc[:, 512 * g + S:512 * g + 2 * S],
                                        scalar=now[:, NOW_POOL + g:NOW_POOL + g + 1],
                                        in1=y_high[:, g, :].bitcast(F32), op0=ALU.mult, op1=ALU.subtract
                                    ).then_inc(pool_ready.sem, 1)
                            if k == 7:
                                merge(7, 1, 0, 16, first=True)
                            if kind in "qk":
                                i = head_no(k)
                                dve.wait_ge(head_sq.sem, head_sq.at(at, i + 1))
                                nc.vector.tensor_copy(flat(proj[:, 2 * i:2 * i + 2, :]), pair[q % 2][:, :]
                                                      ).then_inc(pair_free[q % 2].sem, 1)
                            if kind == "v":
                                i = k - 12 if k < 14 else k - 18 + 4
                                product_ready(k)
                                nc.vector.tensor_copy(tok[:, :, 256 * i:256 * i + 256],
                                                      pair[q % 2][:, :].rearrange("p (t n) -> p t n", t=2)
                                                      ).then_inc(pair_free[q % 2].sem, 1)
                            if k in (12, 18):
                                group = (k - 12) // 6
                                w = slice(S * group, S * group + S)
                                dve.wait_ge(head_root.sem, head_root.at(at, group + 1))
                                nc.vector.reciprocal(rstd[0:16, w], root[0:16, w]).then_inc(head_rstd.sem, 1)
                            if k in (13, 19):
                                group = (k - 13) // 6
                                dve.wait_ge(head_spread.sem, head_spread.at(at, group + 1))
                                for i in range(4 * group, 4 * group + 4):
                                    w = flat(proj[:, 2 * i:2 * i + 2, :])
                                    gain = NOW_QK + i // 2
                                    bank = 512 * (i % 4)
                                    nc.vector.scalar_tensor_tensor(
                                        out=w, in0=w, scalar=now[:, gain:gain + 1],
                                        in1=acc[:, bank:bank + 512], op0=ALU.mult, op1=ALU.mult
                                    ).then_inc(head_normed.sem, 1)
                            if k == 9:
                                dve.wait_ge(f_split.sem, f_split.at(at, 1))
                                nc.vector.tensor_tensor(flat(f_low[:, :, :]), flat(f_raw[:, :, :]),
                                                        flat(f_high[:, :, :]).bitcast(F32), ALU.subtract
                                                        ).then_inc(f_split.sem, 1)
                            q += kind not in ROW_KINDS
                        dve.wait_ge(f_done.sem, f_done.at(at, 1))
                        linked(nc.vector.tensor_tensor(f_val[:, :, :], small[:, 16:32].rearrange("p (t h) -> p t h", t=TT),
                                                       f_bias[:, l, :].unsqueeze(1).to_broadcast([P, TT, 8]),
                                                       ALU.add), at)
                        linked(nc.vector.scalar_tensor_tensor(
                            out=flat(f_abs[:, :, :]), in0=flat(f_val[:, :, :]), scalar=-1.0,
                            in1=flat(f_val[:, :, :]), op0=ALU.mult, op1=ALU.max), at)
                        dve.wait_ge(step_act.sem, step_act.at(at, 2))
                        nc.vector.scalar_tensor_tensor(
                            out=flat(logf[:, :, :]), in0=flat(f_val[:, :, :]), scalar=0.0,
                            in1=flat(f_abs[:, :, :]), op0=ALU.min, op1=ALU.subtract).then_inc(f_ready.sem, 1)
                        attention_dve()
                        low(at, MIX + 30, 0)
                        unit(27)
                        low(at, MIX + 31, 1)
                        merge(29, 2, 4, 16, gates=1)
                        low(at, MIX + 32, 2)
                        merge(31, 3, 8, 24, gates=2, last=True)
                        low(at, MIX + 33, 0)
                        first_out, a_out = 32, 4
                    else:
                        nc.vector.memset(conv_u()[:, :, 0:2], 0.0)
                        for k, (kind, a) in enumerate(MIX2):
                            if kind == "g":
                                break
                            low(at, MIX + k + 2, (k + 2) % 3)
                            unit(k)
                            if kind == "ch":
                                i = k // 2
                                wait_taken(dve, at, b, k - 1)
                                product_ready(k)
                                nc.vector.tensor_tensor(conv_u()[:, 2 * i:2 * i + 2, 2:2 + S],
                                                        temp[:, 0:512].rearrange("p (a n) -> p a n", a=2),
                                                        pair[q % 2][:, :].rearrange("p (a n) -> p a n", a=2),
                                                        ALU.mult).then_inc(pair_free[q % 2].sem, 1)
                            if kind == "cb":
                                i = k - 8
                                wait_taken(dve, at, b, 7)
                                if i >= 1:
                                    dve.wait_ge(conv_split.sem, conv_split.at(at, i))
                                for tap in range(3):
                                    for a2 in range(2):
                                        d = 2 * i + a2
                                        dst = temp[:, S * a2:S * a2 + S]
                                        u = conv_u()[:, d, tap:tap + S]
                                        w = now[:, NOW_CONV + 8 * tap + d:NOW_CONV + 8 * tap + d + 1]
                                        if tap == 0:
                                            ins = nc.vector.tensor_scalar(dst, u, w, None, ALU.mult)
                                        else:
                                            ins = nc.vector.scalar_tensor_tensor(out=dst, in0=u, scalar=w, in1=dst,
                                                                                 op0=ALU.mult, op1=ALU.add)
                                    if tap < 2:
                                        linked(ins, at)
                                ins.then_inc(conv_ready.sem, 1)
                                dve.wait_ge(conv_ready.sem, conv_ready.at(at, i + 1))
                                product_ready(k)
                                nc.vector.tensor_tensor(temp[:, 512:1024], temp[:, 0:512], pair[q % 2][:, :],
                                                        ALU.mult).then_inc(pair_free[q % 2].sem, 1)
                                dve.wait_ge(conv_high.sem, conv_high.at(at, i + 1))
                                nc.vector.tensor_tensor(flat(y_low[:, 2 * i:2 * i + 2, :]), temp[:, 512:1024],
                                                        flat(y_high[:, 2 * i:2 * i + 2, :]).bitcast(F32),
                                                        ALU.subtract).then_inc(conv_split.sem, 1)
                            if k == 19:
                                merge(19, 1, 0, 24, first=True)
                            q += kind not in ROW_KINDS
                        attention_dve()
                        low(at, MIX + 44, 2)
                        merge(43, 2, 4, 24, gates=1, last=True)
                        low(at, MIX + 45, 0)
                        first_out, a_out = 44, 3
                    for k in range(first_out, first_out + 3):
                        low(at, MIX + k + 2, (k + 2) % 3)
                        if b == 0 and k <= 33:
                            unit(k)
                    update(at, MIX + MIX_CHUNKS[b] - 1, a_out)
                    assert links[0] == chain.per[b], links
                    ffn_dve(1)

            dve.wait_ge(root_ready.sem, root_ready.at("end", 1))
            nc.vector.reciprocal(rstd[:, 0:S], root[:, 0:S]).then_inc(rstd_ready.sem, 1)
            dve.wait_ge(rstd_ready.sem, rstd_ready.at("end", 1))
            for d in range(DT):
                nc.vector.scalar_tensor_tensor(out=work[:, d, :], in0=x[:, d, :],
                                               scalar=params[:, GAIN + 96 + d:GAIN + 97 + d],
                                               in1=rstd[:, 0:S], op0=ALU.mult, op1=ALU.mult
                                               ).then_inc(scaled_ready.sem, 1)
            dve.wait_ge(result_turned.sem, 1)
            for bank in range(4):
                nc.vector.tensor_copy(proj_f[:, 512 * bank:512 * bank + 512], acc[:, 512 * bank:512 * bank + 512]
                                      ).then_inc(result_ready.sem, 1)

        @block.tensor
        def _(pe):
            mm = nc.tensor.matmul

            def triple(dst, a_h, a_l, b_h, b_l, start):
                mm(dst, a_h, b_h, start=start, stop=False, skip_group_check=True)
                mm(dst, a_h, b_l, start=False, stop=False, skip_group_check=True)
                return mm(dst, a_l, b_h, start=False, stop=True, skip_group_check=True)

            def column(at, n, q, slot, token_major=False, stage=None, extra=None, q_extra=None,
                       tiles=(0, 1)):
                free = pair_free[q % 2]
                if 0 in tiles:
                    pe.wait_ge(w_low_ready.sem, w_low_ready.at(at, n + 1, extra))
                    pe.wait_ge(free.sem, free.at(at, q // 2, q_extra))
                wh, wl = cols3(w_high[:, slot, :]), cols3(w_low[:, slot, :])
                for k in range(DT):
                    if stage is not None:
                        pe.wait_ge(h_ready.sem, h_ready.at(at, DT * stage + k + 1))
                    for i in tiles:
                        dst = pair[q % 2][:, S * i:S * i + S]
                        c = slice(P * i, P * i + P)
                        if token_major:
                            last = triple(dst, h_high[:, k, c], h_low[:, k, c], wh[:, k, :], wl[:, k, :],
                                          k == 0 and i == 0)
                        else:
                            last = triple(dst, wh[:, k, c], wl[:, k, c], h_high[:, k, :], h_low[:, k, :],
                                          k == 0 and i == 0)
                if 1 in tiles:
                    last.then_inc(chunk_used.sem, 1)

            def row(at, n, slot, src_h, src_l, tiles, start=False, last=False, extra=None, banks=None):
                pe.wait_ge(w_low_ready.sem, w_low_ready.at(at, n + 1, extra))
                wh, wl = rows3(w_high[:, slot, :]), rows3(w_low[:, slot, :])
                for d in range(DT):
                    for kk in range(2):
                        if banks is not None and kk == 0 and d % 2 == 0:
                            pe.wait_ge(acc_taken.sem, acc_taken.at(at, banks + d // 2 + 1))
                        c = slice(P * d, P * d + P)
                        ins = triple(acc[:, S * d:S * d + S], wh[:, kk, c], wl[:, kk, c],
                                     src_h[:, tiles[kk], :], src_l[:, tiles[kk], :],
                                     start and kk == 0 and d % 2 == 0)
                        if last and kk == 1 and d % 2 == 1 and d < DT - 1:
                            ins.then_inc(acc_done.sem, 1)
                ins.then_inc(chunk_used.sem, 1)

            def clear_acc():
                for bank in [*range(4)] * 3:
                    mm(acc[:, 512 * bank:512 * bank + 512], zeros[0:1, 0:P], zeros[0:1, :], start=True,
                       stop=True, skip_group_check=True)

            def first_ada(u):
                slot, landed = first_slots[u % FIRST_RING]
                pe.wait_ge(ada_copied.sem, u + 2)
                w = cols3(slot)
                if u in FIRST_SUMMED:
                    pe.wait_ge(ada_part.sem, DT * (FIRST_SUMMED.index(u) + 1))
                    tiles = [(0, ones[:, :])]
                else:
                    pe.wait_ge(landed.sem, 16 * (u // FIRST_RING + 1))
                    tiles = [(k, c_act[:, 0, k:k + 1]) for k in range(DT)]
                for i in range(2):
                    for k, factor in tiles:
                        last = mm(small[:, 2 * (u % 2) + i:2 * (u % 2) + i + 1], w[:, k, P * i:P * i + P], factor,
                                  start=k == 0, stop=k == tiles[-1][0], skip_group_check=True)
                last.then_inc(ada_used.sem, 1)

            def ada(at, u, slot, part_extra=None, extra=None):
                pe.wait_ge(ada_part.sem, ada_part.at(at, DT * (u + 1), part_extra))
                pe.wait_ge(ada_copied.sem, ada_copied.at(at, u, extra))
                for i in range(2):
                    last = mm(small[:, 2 * slot + i:2 * slot + i + 1], ada_raw[:, slot, P * i:P * i + P],
                              ones[:, :], start=True, stop=True, skip_group_check=True)
                last.then_inc(ada_used.sem, 1)

            def mean_square(at, s):
                for d in range(DT):
                    pe.wait_ge(squares_ready.sem, squares_ready.at(at, DT * s + d + 1))
                    last = mm(stat[:, 0:S], mean_all, work[:, d, :], start=d == 0, stop=d == DT - 1)
                last.then_inc(stat_done.sem, 1)

            pe.sem_inc(chunk_used.sem, 3)
            pe.sem_inc(w_low_ready.sem, 3)
            pe.sem_inc(ada_used.sem, 2)
            pe.sem_inc(ada_copied.sem, 2)
            for free in pair_free:
                pe.sem_inc(free.sem, 1)
            pe.wait_ge(const_landed.sem, 48)
            pe.wait_ge(rows_landed.sem, 80)
            stage_rows = flat(proj[:, 16:24, :])
            nc.tensor.transpose(pair[0][:, 0:120], stage_rows[0:120, 0:P], ident[0:120, 0:120])
            nc.tensor.transpose(pair[0][:, 120:184], stage_rows[0:64, P:2 * P], ident[0:64, 0:64])
            for i in range(3):
                last = nc.tensor.transpose(pair[1][:, 96 * i:96 * i + 96], stage_rows[0:96, (2 + i) * P:(3 + i) * P],
                                           ident[0:96, 0:96])
            last.then_inc(params_turned.sem, 1)
            pe.wait_ge(c_ready.sem, 5)
            pe.wait_ge(zeros_ready.sem, 3)
            for u in range(UNITS):
                first_ada(u)
                if u == 2:
                    pe.wait_ge(table_landed.sem, 80)
                    mm(stat[0:24, 0:TAB], proj_f[0:32, TAB:TAB + 24], proj_f[0:32, 2 * TAB:3 * TAB], start=True,
                       stop=True).then_inc(params_turned.sem, 1)
                    pe.wait_ge(x_landed.sem, 16)
                    for d in range(DT):
                        for tt in range(TT):
                            last = nc.tensor.transpose(acc[:, S * d + P * tt:S * d + P * tt + P],
                                                       work_f[:, D * tt + P * d:D * tt + P * d + P], ident)
                    last.then_inc(x_turned.sem, 1)

            for b in range(2):
                with pe.Fori(0, DEPTH) as l:
                    at = (b, l)

                    def ffn_pe(i):
                        stage, c = 2 * i, i * (MIX + MIX_CHUNKS[b])
                        q0 = i * (COLS[b] - 2 * TRIPS)
                        y0 = 11 * i
                        mean_square(at, stage)
                        clear_acc()
                        column(at, c, q0, 0, stage=stage)
                        column(at, c + 1, q0 + 1, 1)
                        ada(at, 12 * stage, 0)
                        with pe.Fori(0, (TRIPS - 1) // 2) as r:
                            for half in range(2):
                                j = 1 + half
                                column(at, c + 3 * j - 1, q0 + 2 * j, 2, extra=r * 6, q_extra=r * 2)
                                column(at, c + 3 * j, q0 + 2 * j + 1, 0, extra=r * 6, q_extra=r * 2)
                                pe.wait_ge(hidden_split.sem, hidden_split.at(at, y0 + j, r * 2))
                                e = 2 * ((j - 1) % 2)
                                row(at, c + 3 * j + 1, 1, y_high, y_low, (e, e + 1), extra=r * 6)
                                ada(at, 12 * stage + j, j % 2, r * 16, r * 2)
                        pe.wait_ge(hidden_split.sem, hidden_split.at(at, y0 + TRIPS))
                        row(at, c + FFN_CHUNKS - 1, 2, y_high, y_low, (0, 1), last=True)
                        ada(at, 12 * stage + UNITS - 1, 1)

                    def attention_pe(q_first):
                        G = GROUPS2 if b else 1

                        def head(m):
                            h = m % 8
                            return h, slice(HEAD * (h % 2), HEAD * (h % 2) + HEAD)

                        def scores(m):
                            forget = m >= 8
                            h, rows_ = head(m)
                            if m >= (1 if b else 2):
                                pe.wait_ge(logits_ready.sem, logits_ready.at(at, 2 * (m if b else m - 1)))
                            for half, dst in enumerate(score_places(b, m)):
                                w = P * (1 + half)
                                for g in range(G):
                                    qt, kt = (4 * g, 12 + 4 * g) if b else ((8, 12) if forget else (0, 4))
                                    last = mm(dst[:, w * g:w * g + w], proj[rows_, qt + h // 2, P * half:P * half + P],
                                              proj[rows_, kt + h // 2, 0:w], start=True, stop=not forget,
                                              skip_group_check=True)
                                if forget:
                                    last = mm(dst[:, 0:w], ident[0:8, h:h + 1].to_broadcast([8, P]), cum_k[:, 0:w],
                                              start=False, stop=True, skip_group_check=True)
                                last.then_inc(scores_done.sem, 1)

                        def turn(m):
                            wide, o = P * G, 0 if b else 576 * (m % 2)
                            for part in range(TURNS[b]):
                                n = TURNS[b] * m + part
                                if part < 2:
                                    pe.wait_ge(probs_ready.sem, probs_ready.at(at, 2 * m + (part + 1 if b else 2)))
                                if n >= 2:
                                    pe.wait_ge(turned_ready.sem, turned_ready.at(at, n - 1))
                                for j, g3 in enumerate((part,) if b else (0, 1, 2)):
                                    for g in range(G):
                                        c = o + (P * g if g3 == 0 else wide + S * g + P * (g3 - 1))
                                        d = wide * j + P * g
                                        last = nc.tensor.transpose(turned[n % 2][:, d:d + P], temp[:, c:c + P], ident)
                                last.then_inc(turned_done.sem, 1)

                        def values(m):
                            h, _ = head(m)
                            wide, o = P * G, 0 if b else 576 * (m % 2)
                            if m == 0:
                                pe.wait_ge(ada_copied.sem, ada_copied.at(at, 12 + UNITS - (3, 0)[b]))
                            else:
                                pe.wait_ge(y_ready.sem, y_ready.at(at, m))
                            pe.wait_ge(turned_ready.sem, turned_ready.at(at, TURNS[b] * (m + 1)))
                            base = 1024 if m >= 8 else 0
                            for half in range(2):
                                parts = [(0, 0)] if half == 0 else [(0, 1), (1, 2)]
                                todo = [(g, kt, g3) for kt, g3 in parts for g in range(G)]
                                for j, (g, kt, g3) in enumerate(todo):
                                    c = (512 * g if b else base) + P * (h // 2)
                                    p0 = o + wide * g3 + P * g
                                    last = mm(small[:, S + P * half:S + P * half + P], tok[:, kt, c:c + P],
                                              probs_t[:, p0:p0 + P],
                                              start=j == 0, stop=j == len(todo) - 1, skip_group_check=True)
                            last.then_inc(out_done.sem, 1)

                        def log_sums():
                            pe.wait_ge(f_ready.sem, f_ready.at(at, 1))
                            pe.wait_ge(y_ready.sem, y_ready.at(at, 4 - VALUE_STEP[b]))
                            mm(small[:, 32:40], upto[:, 0:P], logf[:, 0, :], start=True, stop=True,
                               skip_group_check=True)
                            mm(small[:, 40:48], upto[:, P:S], logf[:, 0, :], start=True, stop=False,
                               skip_group_check=True)
                            mm(small[:, 40:48], upto[:, 0:P], logf[:, 1, :], start=False, stop=True,
                               skip_group_check=True).then_inc(cum_done.sem, 1)
                            mm(small[0:8, S:2 * S], logf[:, 0, :], upto, start=True, stop=False, skip_group_check=True)
                            mm(small[0:8, S + P:2 * S], logf[:, 1, :], upto[:, 0:P], start=False, stop=True,
                               skip_group_check=True).then_inc(cum_done.sem, 1)

                        count = HEADS[b]
                        for i in range(count + VALUE_STEP[b]):
                            if not b and i >= 2 and i - 2 < count:
                                turn(i - 2)
                            if not b and i == 4:
                                log_sums()
                            if i < count:
                                scores(i)
                            if not b and i == 4:
                                pe.wait_ge(cum_ready.sem, cum_ready.at(at, 2))
                            if i >= VALUE_STEP[b]:
                                values(i - VALUE_STEP[b])
                            if b and 1 <= i <= count:
                                turn(i - 1)
                            if i < count:
                                column(at, MIX + GATES_FROM[b] + i // 2, q_first + i // 2,
                                       (GATES_FROM[b] + i // 2) % 3, tiles=(i % 2,))

                    def unit(k):
                        u = unit_behind(b, k)
                        if u is not None:
                            ada(at, 12 + u, u % 2)

                    ffn_pe(0)
                    mean_square(at, 1)
                    clear_acc()
                    q = 2 * TRIPS
                    if b == 0:
                        for k, (kind, a) in enumerate(MIX1):
                            if kind == "g":
                                break
                            if kind == "wb":
                                if k == 6:
                                    pe.wait_ge(pool_ready.sem, pool_ready.at(at, 4))
                                i = k - 6
                                row(at, MIX + k, k % 3, y_high, y_low, (2 * i, 2 * i + 1), start=i == 0, last=i == 1)
                            else:
                                column(at, MIX + k, q, k % 3, kind in TOKEN_KINDS, 1 if k == 0 else None)
                                q += 1
                            if k == 2:
                                wait_taken(pe, at, b, 0)
                                wait_taken(pe, at, b, 1)
                                pe.wait_ge(side_landed.sem, side_landed.at(at, 48))
                                for g in range(4):
                                    mm(acc[:, 512 * g:512 * g + S], tok[:, 0, 512 + P * g:512 + P * g + P],
                                       proj_f[:, 384 * g:384 * g + S], start=True, stop=False, skip_group_check=True)
                                    last = mm(acc[:, 512 * g + P:512 * g + S], tok[:, 1, 512 + P * g:512 + P * g + P],
                                              proj_f[:, 384 * g + S:384 * g + S + P], start=False, stop=True,
                                              skip_group_check=True)
                                last.then_inc(pool_d_done.sem, 1)
                            if k == 3:
                                for g in range(4):
                                    pe.wait_ge(pool_d_ready.sem, pool_d_ready.at(at, g + 1))
                                    last = mm(acc[:, 512 * g + S:512 * g + 2 * S], proj_f[:, 1536 + P * g:1536 + P * g + P],
                                              proj[:, 8 + g, :], start=True, stop=True, skip_group_check=True)
                                last.then_inc(pool_y_done.sem, 1)
                            if k >= 1 and MIX1[k - 1][0] in "qk":
                                i = head_no(k - 1)
                                group, t0 = i // 4, 2 * (i % 4)
                                pe.wait_ge(head_sq.sem, head_sq.at(at, i + 1))
                                for a2 in range(2):
                                    last = mm(stat[0:16, S * group:S * group + S], head_means(t0 + a2),
                                              temp[:, S * a2:S * a2 + S], start=t0 + a2 == 0, stop=t0 + a2 == 7,
                                              skip_group_check=True)
                                last.then_inc(head_stat.sem, 1)
                            if k in (13, 19):
                                group = (k - 13) // 6
                                pe.wait_ge(head_rstd.sem, head_rstd.at(at, group + 1))
                                if group == 0:
                                    pe.wait_ge(acc_taken.sem, acc_taken.at(at, 4))
                                else:
                                    pe.wait_ge(head_normed.sem, head_normed.at(at, 4))
                                for t_ in range(8):
                                    last = mm(acc[:, S * t_:S * t_ + S],
                                              head_spread_of(t_),
                                              rstd[0:16, S * group:S * group + S], start=True, stop=True,
                                              skip_group_check=True)
                                last.then_inc(head_spread.sem, 1)
                            unit(k)
                        pe.wait_ge(f_split.sem, f_split.at(at, 2))
                        pe.wait_ge(ada_copied.sem, ada_copied.at(at, 12 + 9))
                        for tt in range(TT):
                            for k in range(DT):
                                c = slice(P * tt, P * tt + P)
                                last = triple(small[:, 16 + 8 * tt:24 + 8 * tt], h_high[:, k, c], h_low[:, k, c],
                                              f_high[:, k, :], f_low[:, k, :], tt == 0 and k == 0)
                        last.then_inc(f_done.sem, 1)
                        pe.wait_ge(head_normed.sem, head_normed.at(at, 8))
                        wait_taken(pe, at, b, 18)
                        wait_taken(pe, at, b, 19)
                        attention_pe(q)
                        pe.wait_ge(y_ready.sem, y_ready.at(at, 16))
                        for i in range(2):
                            row(at, MIX + 28 + i, (28 + i) % 3, y_high, y_low, (2 * i, 2 * i + 1),
                                start=i == 0, last=i == 1)
                            unit(28 + i)
                        for i in range(2):
                            row(at, MIX + 30 + i, (30 + i) % 3, y_high, y_low, (4 + 2 * i, 5 + 2 * i),
                                start=i == 0, last=i == 1, banks=4 if i == 0 else None)
                            unit(30 + i)
                        first_out, taken = 32, 8
                    else:
                        for k, (kind, a) in enumerate(MIX2):
                            if kind == "g":
                                break
                            if kind == "wconv":
                                i = k - 16
                                if i == 0:
                                    pe.wait_ge(conv_split.sem, conv_split.at(at, 4))
                                row(at, MIX + k, k % 3, y_high, y_low, (2 * i, 2 * i + 1), start=i == 0, last=i == 3)
                            else:
                                column(at, MIX + k, q, k % 3, kind in TOKEN_KINDS, 1 if k == 0 else None)
                                q += 1
                            unit(k)
                        wait_taken(pe, at, b, 36)
                        wait_taken(pe, at, b, 37)
                        pe.wait_ge(acc_taken.sem, acc_taken.at(at, 4))
                        attention_pe(q)
                        pe.wait_ge(y_ready.sem, y_ready.at(at, 8))
                        for i in range(2):
                            row(at, MIX + 42 + i, (42 + i) % 3, y_high, y_low, (2 * i, 2 * i + 1),
                                start=i == 0, last=i == 1)
                            unit(42 + i)
                        first_out, taken = 44, 4
                    for i in range(4):
                        pe.wait_ge(out_split.sem, out_split.at(at, i + 1))
                        row(at, MIX + first_out + i, (first_out + i) % 3, h_high, h_low, (2 * i, 2 * i + 1),
                            start=i == 0, last=i == 3, banks=taken if i == 0 else None)
                        unit(first_out + i)
                    ffn_pe(1)

            mean_square("end", 0)
            for d in range(DT):
                pe.wait_ge(scaled_ready.sem, scaled_ready.at("end", d + 1))
                for tt in range(TT):
                    last = nc.tensor.transpose(acc[:, D * tt + P * d:D * tt + P * d + P],
                                               work[:, d, P * tt:P * tt + P], ident)
            last.then_inc(result_turned.sem, 1)


def constants():
    const = np.zeros((P, CONSTS), np.float32)
    const[:, ID:ID + P] = np.eye(P)
    const[:, ONES:ONES + P] = 1.0 / D
    const[:, BLOCK:BLOCK + 32] = (np.arange(P)[:, None] // HEAD + 14 == np.arange(32)[None, :]) / HEAD
    const[:, UPTO:UPTO + S] = np.arange(P)[:, None] <= np.arange(S)[None, :]
    const[:, CAUSAL + P:CAUSAL + S] = np.where(np.arange(P)[None, :] > np.arange(P)[:, None], NEG, 0.0)

    token = np.arange(S)
    pool = np.zeros((P, 4, 384), np.float32)
    for g, w in enumerate(POOL_W):
        back = token[None, :] - token[:, None]
        m = ((back >= 0) & (back < w)) / np.minimum(token + 1, w)[None, :] - (back == 0)
        pool[:, g, 0:S] = m[0:P, :]
        pool[:, g, S:384] = m[P:S, P:S]

    exact = 16
    dist = 255 - np.arange(TAB)
    far = np.maximum(dist, 1).astype(np.float32)
    large = exact + (np.log(far / exact) / np.log(2048 / exact) * (32 - exact)).astype(np.int32)
    bucket = np.where(dist < exact, np.maximum(dist, 0), np.minimum(large, 31)).astype(np.int32)
    one_hot = np.zeros((32, TAB), np.float32)
    mask = np.full((24, TAB), NEG, np.float32)
    for g, (window, step) in enumerate(((128, 1), (512, 4), (2048, 16))):
        seen = (dist >= 0) & (dist % step == 0) & (dist <= window)
        for half in range(2):
            mask[12 * half + 4 * g:12 * half + 4 * g + 4, seen] = 0.0
    one_hot[bucket[dist >= 0], np.arange(TAB)[dist >= 0]] = 1.0
    return const, pool.reshape(P, 1536), one_hot, mask


def kernel(**inputs):
    import concourse.bacc as _bacc
    from concourse.bass_utils import run_bass_kernel_spmd as _run

    a = {k: np.asarray(v) for k, v in inputs.items()}
    row = lambda *parts: np.concatenate([np.ascontiguousarray(p).reshape(-1, P) for p in parts])
    const, pool, one_hot, mask = constants()
    gains = np.repeat(a["qk_gain"].reshape(8, 1, HEAD), 2, axis=1)
    arrays = {
        "x": a["x"],
        "w_ada_all": np.concatenate([a["w_ada"], a["ada_w_2"]]),
        "ffn_gate_all": np.concatenate([a["ffn_w_gate"], a["ffn_w_gate_2"]]),
        "ffn_up_all": np.concatenate([a["ffn_w_up"], a["ffn_w_up_2"]]),
        "ffn_down_all": np.concatenate([a["ffn_w_down"], a["ffn_w_down_2"]]),
        "w_in": a["w_in"], "w_in_2": a["w_in_2"], "w_branch": a["w_branch"], "w_out": a["w_out"],
        "w_pool": a["w_pool"], "forget_bias": a["forget_bias"], "rel_bias_2": a["rel_bias_2"].reshape(32, 3, 2, 4).transpose(0, 2, 1, 3).reshape(32, 24).copy(),
        "w_conv_out_2": a["w_conv_out_2"], "w_attn_out_2": a["w_attn_out_2"], "w_o_2": a["w_o_2"],
        "rel_rows": np.ascontiguousarray(a["rel_bias"].reshape(16, REL)[:, ::-1]),
        "rows_a": row(a["norm_gain"], a["norm_g_2"], a["final_g_2"], gains, a["pool_scale"]),
        "rows_b": row(a["conv_w_2"], a["c"], a["c_2"]),
        "rows_ada": row(a["b_ada"], a["ada_b_2"]),
        "const": const, "pool_mats": pool, "one_hot": one_hot, "distance_mask": mask,
        "head_rows": np.repeat(np.eye(16, dtype=np.float32), HEAD, axis=1),
    }
    nc = _bacc.Bacc("TRN2", target_bir_lowering=False, num_devices=1)
    tensors = {n: nc.dram_tensor(f"in_{n}", v.shape, F32, kind="ExternalInput").ap() for n, v in arrays.items()}
    out = nc.dram_tensor("out_0", (1, S, D), F32, kind="ExternalOutput").ap()
    build(nc, tensors, out)
    r = _run(nc, [{f"in_{n}": v for n, v in arrays.items()}], core_ids=[0])
    return r.results[0]["out_0"]
```
